# Optimizing a Trainium2 kernel written in Bass

```python
import math
import jax, jax.numpy as jnp
from jax import lax
import numpy as np

D_MODEL = 2048
BATCH = 1
SEQ = 512
DEPTH = 2

N_MIXERS = 2
N_MLA = (DEPTH + 1) // 2
N_SSD = DEPTH // 2

ALPHA = (2 * DEPTH) ** 0.25
BETA = (8 * DEPTH) ** -0.25

PLE_DIM = 256

MLA_HEADS = 16
Q_LORA = 512
KV_LORA = 512
QK_NOPE = 128
QK_ROPE = 64
V_HEAD = 128
QK_HEAD = QK_NOPE + QK_ROPE
MLA_WIDTH = MLA_HEADS * V_HEAD
MLA_IN_DIM = Q_LORA + KV_LORA + QK_ROPE + MLA_WIDTH
ROPE_BASE = 10000.0
Q_BLOCK = 128
ATTN_SCALE = QK_HEAD ** -0.5

EXPAND = 2
D_INNER = EXPAND * D_MODEL
SSD_HEAD_DIM = 64
SSD_HEADS = D_INNER // SSD_HEAD_DIM
N_GROUPS = 8
HEADS_PER_GROUP = SSD_HEADS // N_GROUPS
D_STATE = 128
D_CONV = 7
CONV_DIM = D_INNER + 2 * N_GROUPS * D_STATE
SSD_IN_DIM = D_INNER + CONV_DIM + 2 * SSD_HEADS
CHUNK = 128

LN_EPS = 1e-5
RMS_EPS = 1e-6

kernel_name = "hybrid_mla_ssd_deepnorm_encoder"

def _layernorm(x, g, b):
    xf = x.astype(jnp.float32)
    mu = jnp.mean(xf, axis=-1, keepdims=True)
    var = jnp.mean(jnp.square(xf - mu), axis=-1, keepdims=True)
    return ((xf - mu) * lax.rsqrt(var + LN_EPS) * g + b).astype(x.dtype)

def _rmsnorm(x, g):
    xf = x.astype(jnp.float32)
    return (xf * lax.rsqrt(jnp.mean(jnp.square(xf), axis=-1, keepdims=True) + RMS_EPS) * g).astype(x.dtype)

def _rope(t, cos, sin):
    t1, t2 = jnp.split(t.astype(jnp.float32), 2, axis=-1)
    return jnp.concatenate([t1 * cos - t2 * sin, t2 * cos + t1 * sin], axis=-1).astype(t.dtype)

def _mla_attention(q_nope, q_rope, k_nope, k_rope, v):
    b, s, h, _ = q_nope.shape
    nb = s // Q_BLOCK

    def block(args):
        qn, qr = args
        sc = (jnp.einsum('bqhd,bkhd->bhqk', qn, k_nope)
              + jnp.einsum('bqhr,bkr->bhqk', qr, k_rope)).astype(jnp.float32) * ATTN_SCALE
        pr = jax.nn.softmax(sc, axis=-1).astype(v.dtype)
        return jnp.einsum('bhqk,bkhd->bqhd', pr, v)

    qn = q_nope.reshape(b, nb, Q_BLOCK, h, QK_NOPE).swapaxes(0, 1)
    qr = q_rope.reshape(b, nb, Q_BLOCK, h, QK_ROPE).swapaxes(0, 1)
    o = lax.map(block, (qn, qr))
    return o.swapaxes(0, 1).reshape(b, s, h * V_HEAD)

def _mla_mixer(x, cos, sin, w_in, q_norm, kv_norm, w_uq, w_ukv, w_o):
    b, s, _ = x.shape
    h = x @ w_in
    c_q = h[..., :Q_LORA]
    c_kv = h[..., Q_LORA:Q_LORA + KV_LORA]
    k_r = h[..., Q_LORA + KV_LORA:Q_LORA + KV_LORA + QK_ROPE]
    z = h[..., Q_LORA + KV_LORA + QK_ROPE:]
    q = (_rmsnorm(c_q, q_norm) @ w_uq).reshape(b, s, MLA_HEADS, QK_HEAD)
    q_nope, q_rope = q[..., :QK_NOPE], _rope(q[..., QK_NOPE:], cos[:, :, None], sin[:, :, None])
    kv = (_rmsnorm(c_kv, kv_norm) @ w_ukv).reshape(b, s, MLA_HEADS, QK_NOPE + V_HEAD)
    k_nope, v = kv[..., :QK_NOPE], kv[..., QK_NOPE:]
    k_rope = _rope(k_r, cos, sin)
    o = _mla_attention(q_nope, q_rope, k_nope, k_rope, v)
    return (o * jax.nn.silu(z)) @ w_o

def _ssd_scan(xs, dt, a_neg, bm, cm):
    b, s = xs.shape[:2]
    nc = s // CHUNK
    G, Hg, P, N = N_GROUPS, HEADS_PER_GROUP, SSD_HEAD_DIM, D_STATE
    X = (xs.astype(jnp.float32) * dt[..., None]).reshape(b, nc, CHUNK, G, Hg, P).swapaxes(0, 1)
    a = (dt * a_neg).reshape(b, nc, CHUNK, G, Hg).swapaxes(0, 1)
    Bc = bm.astype(jnp.float32).reshape(b, nc, CHUNK, G, N).swapaxes(0, 1)
    Cc = cm.astype(jnp.float32).reshape(b, nc, CHUNK, G, N).swapaxes(0, 1)
    mask = jnp.tril(jnp.ones((CHUNK, CHUNK), dtype=bool))[None, :, :, None, None]

    def step(state, inp):
        xc, ac, bc, cc = inp
        acs = jnp.cumsum(ac, axis=1)
        seg = acs[:, :, None] - acs[:, None, :]
        lmat = jnp.exp(jnp.where(mask, seg, -jnp.inf))
        cb = jnp.einsum('bign,bjgn->bijg', cc, bc)
        y = jnp.einsum('bijg,bijgh,bjghp->bighp', cb, lmat, xc)
        y = y + jnp.einsum('bign,bghpn,bigh->bighp', cc, state, jnp.exp(acs))
        decay_end = jnp.exp(acs[:, -1:] - acs)
        state = (state * jnp.exp(acs[:, -1])[..., None, None]
                 + jnp.einsum('bjgn,bjgh,bjghp->bghpn', bc, decay_end, xc))
        return state, y

    state0 = jnp.zeros((b, G, Hg, P, N), jnp.float32)
    _, ys = lax.scan(step, state0, (X, a, Bc, Cc))
    return ys.swapaxes(0, 1).reshape(b, s, SSD_HEADS, P).astype(xs.dtype)

def _ssd_mixer(x, w_in, conv_w, conv_b, dt_bias, a_log, d_skip, norm_w, w_out):
    b, s, _ = x.shape
    h = x @ w_in
    z = h[..., :D_INNER]
    xbc = h[..., D_INNER:D_INNER + CONV_DIM]
    dt = h[..., D_INNER + CONV_DIM:].reshape(b, s, 2, SSD_HEADS)
    pad = D_CONV // 2
    xbc = lax.conv_general_dilated(xbc, conv_w[:, None, :].astype(xbc.dtype), window_strides=(1,),
                                   padding=[(pad, pad)], dimension_numbers=('NWC', 'WIO', 'NWC'),
                                   feature_group_count=CONV_DIM) + conv_b
    xbc = jax.nn.silu(xbc)
    xs = xbc[..., :D_INNER].reshape(b, s, SSD_HEADS, SSD_HEAD_DIM)
    bm = xbc[..., D_INNER:D_INNER + N_GROUPS * D_STATE].reshape(b, s, N_GROUPS, D_STATE)
    cm = xbc[..., D_INNER + N_GROUPS * D_STATE:].reshape(b, s, N_GROUPS, D_STATE)
    dt = jax.nn.softplus(dt.astype(jnp.float32) + dt_bias.astype(jnp.float32))
    a_neg = -jnp.exp(a_log.astype(jnp.float32))
    y_f = _ssd_scan(xs, dt[:, :, 0], a_neg[0], bm, cm)
    flip = lambda t: jnp.flip(t, axis=1)
    y_b = flip(_ssd_scan(flip(xs), flip(dt[:, :, 1]), a_neg[1], flip(bm), flip(cm)))
    y = (y_f + y_b + xs * d_skip[:, None]).reshape(b, s, D_INNER)
    y = _rmsnorm(y * jax.nn.silu(z), norm_w)
    return y @ w_out

def setup_inputs(seed: int = 0) -> dict:
    key = jax.random.key(seed)
    ks = jax.random.split(key, 24)
    nrm = lambda k, shape, scale: jax.random.normal(k, shape, jnp.float32) * scale
    x = nrm(ks[0], (BATCH, SEQ, D_MODEL), 1.0)
    p = nrm(ks[1], (DEPTH, BATCH, SEQ, PLE_DIM), 1.0)
    positions = jnp.broadcast_to(jnp.arange(SEQ, dtype=jnp.int32), (BATCH, SEQ))
    ln_g = 1.0 + nrm(ks[2], (DEPTH, D_MODEL), 0.02)
    ln_b = nrm(ks[3], (DEPTH, D_MODEL), 0.02)
    ple_w_proj = nrm(ks[4], (DEPTH, PLE_DIM, D_MODEL), PLE_DIM ** -0.5)
    ple_w_gate = nrm(ks[5], (DEPTH, D_MODEL, D_MODEL), D_MODEL ** -0.5)
    mla_w_in = nrm(ks[6], (N_MLA, D_MODEL, MLA_IN_DIM), D_MODEL ** -0.5)
    mla_q_norm = 1.0 + nrm(ks[7], (N_MLA, Q_LORA), 0.02)
    mla_kv_norm = 1.0 + nrm(ks[8], (N_MLA, KV_LORA), 0.02)
    mla_w_uq = nrm(ks[9], (N_MLA, Q_LORA, MLA_HEADS * QK_HEAD), Q_LORA ** -0.5)
    kv_scale = jnp.tile(jnp.concatenate([jnp.ones((QK_NOPE,), jnp.float32),
                                         jnp.full((V_HEAD,), BETA, jnp.float32)]), MLA_HEADS)
    mla_w_ukv = nrm(ks[10], (N_MLA, KV_LORA, MLA_HEADS * (QK_NOPE + V_HEAD)), KV_LORA ** -0.5) * kv_scale
    mla_w_o = nrm(ks[11], (N_MLA, MLA_WIDTH, D_MODEL), MLA_WIDTH ** -0.5 * BETA)
    ssd_w_in = nrm(ks[12], (N_SSD, D_MODEL, SSD_IN_DIM), D_MODEL ** -0.5)
    ssd_conv_w = nrm(ks[13], (N_SSD, D_CONV, CONV_DIM), D_CONV ** -0.5)
    ssd_conv_b = nrm(ks[14], (N_SSD, CONV_DIM), 0.02)
    u = jax.random.uniform(ks[15], (N_SSD, 2, SSD_HEADS), jnp.float32)
    dt0 = jnp.exp(u * (math.log(0.1) - math.log(0.001)) + math.log(0.001))
    ssd_dt_bias = dt0 + jnp.log(-jnp.expm1(-dt0))
    ssd_a_log = jnp.log(jax.random.uniform(ks[16], (N_SSD, 2, SSD_HEADS), jnp.float32, 1.0, 16.0))
    ssd_d = 1.0 + nrm(ks[17], (N_SSD, SSD_HEADS), 0.02)
    ssd_norm = 1.0 + nrm(ks[18], (N_SSD, D_INNER), 0.02)
    ssd_w_out = nrm(ks[19], (N_SSD, D_INNER, D_MODEL), D_INNER ** -0.5 * BETA)
    return {"x": x, "p": p, "positions": positions, "ln_g": ln_g, "ln_b": ln_b,
            "ple_w_proj": ple_w_proj, "ple_w_gate": ple_w_gate,
            "mla_w_in": mla_w_in, "mla_q_norm": mla_q_norm, "mla_kv_norm": mla_kv_norm,
            "mla_w_uq": mla_w_uq, "mla_w_ukv": mla_w_ukv, "mla_w_o": mla_w_o,
            "ssd_w_in": ssd_w_in, "ssd_conv_w": ssd_conv_w, "ssd_conv_b": ssd_conv_b,
            "ssd_dt_bias": ssd_dt_bias, "ssd_a_log": ssd_a_log, "ssd_d": ssd_d,
            "ssd_norm": ssd_norm, "ssd_w_out": ssd_w_out}

def reference(x, p, positions, ln_g, ln_b, ple_w_proj, ple_w_gate,
              mla_w_in, mla_q_norm, mla_kv_norm, mla_w_uq, mla_w_ukv, mla_w_o,
              ssd_w_in, ssd_conv_w, ssd_conv_b, ssd_dt_bias, ssd_a_log, ssd_d,
              ssd_norm, ssd_w_out):
    inv_freq = 1.0 / (ROPE_BASE ** (jnp.arange(0, QK_ROPE, 2, dtype=jnp.float32) / QK_ROPE))
    ang = positions.astype(jnp.float32)[..., None] * inv_freq
    cos, sin = jnp.cos(ang), jnp.sin(ang)
    for i in range(DEPTH):
        j = i // N_MIXERS
        if i % N_MIXERS == 0:
            h = _mla_mixer(x, cos, sin, mla_w_in[j], mla_q_norm[j], mla_kv_norm[j],
                           mla_w_uq[j], mla_w_ukv[j], mla_w_o[j])
        else:
            h = _ssd_mixer(x, ssd_w_in[j], ssd_conv_w[j], ssd_conv_b[j], ssd_dt_bias[j],
                           ssd_a_log[j], ssd_d[j], ssd_norm[j], ssd_w_out[j])
        x = _layernorm(ALPHA * x + h, ln_g[i], ln_b[i])
        x = x + (p[i] @ ple_w_proj[i]) * jax.nn.sigmoid(x @ ple_w_gate[i])
    return x


_drawn_inputs = setup_inputs


def setup_inputs(seed=0):
    import zlib

    import numpy as np

    out = dict(_drawn_inputs(seed))
    spreads = {}
    factors = {'mla_w_in': 7.492,
     'mla_q_norm': 8.0,
     'mla_kv_norm': 8.0,
     'mla_w_uq': 8.0,
     'mla_w_ukv': 6.107,
     'mla_w_o': 7.527,
     'ssd_conv_b': 7.486,
     'ssd_d': 8.0,
     'ssd_norm': 8.0}
    for name, (base, spread) in spreads.items():
        noise = np.random.default_rng([zlib.crc32(name.encode()), seed]).standard_normal(out[name].shape)
        drawn = base * np.exp(spread * noise) if base else spread * noise
        out[name] = __import__('jax').numpy.asarray(drawn.astype(out[name].dtype))
    for name, factor in factors.items():
        out[name] = (out[name] * factor).astype(out[name].dtype)
    return out
```

```python
from contextlib import ExitStack, contextmanager

import numpy as np
import concourse.bass as bass
from concourse import mybir

F32 = mybir.dt.float32
F32R = mybir.dt.float32r
I32 = mybir.dt.int32
ACT = mybir.ActivationFunctionType
ALU = mybir.AluOpType
AX = mybir.AxisListType

P = 128
D = 2048
SEQ = 512
TT = SEQ // P
KD = D // P
BLK = 512
NB = D // BLK
UNIT = 2048
KU = UNIT // BLK
PLE = 256
HEADS, NOPE, ROPE, VH = 16, 128, 64, 128
QKH = NOPE + ROPE
LORA = 512
KL = LORA // P
SCALE = QKH ** -0.5
ALPHA = 4 ** 0.25
LN_EPS, RMS_EPS = 1e-5, 1e-6
DI = 4096
NH, HD, NG, HG, NS = 64, 64, 8, 8, 128
TAPS = 7
PAD = TAPS // 2
PAIRS = HEADS // 2
GCH = 6
U_CQ, U_CKV, U_KR, U_Z, U_ATT, U_O, U_GATE = 4, 4, 1, 16, 2 * PAIRS, 16, 20
U_DT, U_GRP, U_OUT = 1, 10, 32
UNITS = U_CQ + U_CKV + U_KR + U_Z + U_ATT + U_O + U_GATE + U_DT + NG * U_GRP + U_OUT + U_GATE

TWO_PI_PARTS = (6.28125, 0.0019350051879882812, 3.0199159819567e-07)
ROUND = 12582912.0
PI32 = 3.1415925
AUX2_ATT = TT + 2 + 6 * PAIRS
ORDER_2 = 2 * (1 + GCH * (TAPS - 1) + 8 + 2 + 2 + 6)
AUX_SSD = 3 * 4 * TT + 2 * KL + 1 + PAIRS * 19 + 2 + 3
AUX0_SSD = 3 * TT + 3 + 1 + NB + 1


def group_fills(products, ssd):
    f = []
    for j in range(U_GRP):
        if products and j >= 5:
            f.append((j, ("ctr", j - 5), 2 if j % 2 else 0))
        if ssd:
            if 1 <= j <= 8:
                f.append((j, ("intra", j - 1), 3))
            if j == 0:
                f += [(j, ("back", 3), 1), (j, ("back", 2), 2), (j, ("cb", 0), 0)]
            if j == 1:
                f += [(j, ("back", 1), 1), (j, ("cb", 1), 0)]
            if j in (3, 5, 7):
                f.append((j, ("forth", (j - 3) // 2), 1))
            if j in (2, 4, 6, 8):
                c = (j - 2) // 2
                f += [(j, ("from_f", c), 1)] * (c > 0) + [(j, ("from_b", c), 2)] * (c < TT - 1)
            if j in (3, 5, 7, 9):
                f.append((j, ("ytr", (j - 3) // 2), 0))
            if j in (3, 5):
                f.append((j, ("cb", (j + 1) // 2), 0))
    return f


def bank_no(fills, name):
    bank = next(b for _, n, b in fills if n == name)
    mine = [n for _, n, b in fills if b == bank and not second_half(n)]
    return mine.index(name) + 1


def bank_count(fills, bank):
    return sum(b == bank and not second_half(n) for _, n, b in fills)


def second_half(name):
    return name[0] == "intra" and name[1] % 2 == 1


def fill_no(fills, name):
    return [n for _, n, _ in fills].index(name) + 1


def slot_uses(c):
    first = 16 * (c.n // 2 + 1)
    return first if c.turn is None else c.turn * (8 * c.per) + first


class Count:

    def __init__(self, n=0):
        self.n, self.turn, self.per = n, None, 0

    def at(self, ahead=0):
        v = self.n + ahead
        return v if self.turn is None else self.turn * self.per + v

    def step(self, k=1):
        self.n += k
        return self.at()


@contextmanager
def turns(eng, n, per_turn):
    with eng.Fori(0, n) as turn:
        start = [c.n for c, _ in per_turn]
        for c, per in per_turn:
            c.turn, c.per = turn, per
        yield turn
    for (c, per), first in zip(per_turn, start):
        assert c.n == first + per, (c.n - first, per)
        c.turn, c.n = None, first + n * per


def trunk(nc, x, p, positions, consts, lnw, wstream, small, convw, rows, out):
    base = nc.sbuf_base + (-nc.sbuf_base) % 64

    with ExitStack() as ctx:
        def at(name, kb, shape, dt=F32):
            return nc.alloc_sbuf_tensor_at(name, shape, dt, offset=base + int(kb * 1024))

        def sem(name):
            return ctx.enter_context(nc.semaphore(name))

        xT = [at("xT_hi", 0, [P, KD, SEQ], F32R), at("xT_lo", 32, [P, KD, SEQ], F32R)]
        xtok = at("xtok", 64, [P, TT, D])
        raw = at("raw", 96, [P, 2, UNIT])
        W = [at("w_hi", 112, [P, 2, UNIT], F32R), at("w_lo", 128, [P, 2, UNIT], F32R)]
        ident = at("ident", 144, [P, P])
        mask_le = at("mask_le", 144.5, [P, P])
        mask_ge = at("mask_ge", 145, [P, P])
        smalls = at("smalls", 145.5, [P, 8 + 32])
        stat = at("stat", 146, [P, 256])
        PT = at("PT", 0, [P, 2, TT, SEQ])
        prob = at("prob", 16, [P, 2, SEQ])
        q_tok = at("q_tok", 20, [P, TT, 2, 2, ROPE // 2])
        q_rot = at("q_rot", 22, [P, TT, 2, 2, ROPE // 2])
        rope_a = at("rope_a", 24, [P, TT, 2, ROPE // 2])
        rope_b = at("rope_b", 25, [P, TT, 2, ROPE // 2])
        qrT = at("qrT", 26, [P, 2, SEQ])
        krT = at("krT", 30, [P, SEQ])
        g_raw = at("g_raw", 32, [P, KD, SEQ])
        zT = at("zT", 64, [P, KD, SEQ])
        cT = [at("cT_hi", 148, [P, 2 * KL, SEQ], F32R), at("cT_lo", 164, [P, 2 * KL, SEQ], F32R)]
        qT = at("qT", 180, [P, 2, 2, SEQ])
        kT = at("kT", 188, [P, 2, 2, SEQ])
        v_tok = at("v_tok", 196, [P, 2, TT, 2 * VH])
        cos = at("cos", 204, [P, TT, ROPE // 2])
        sin = at("sin", 204.5, [P, TT, ROPE // 2])
        c_tok = at("c_tok", 180, [P, 2, TT, LORA])
        k_tok = at("k_tok", 196, [P, TT, ROPE])
        k_rot = at("k_rot", 197, [P, TT, 2, ROPE])
        rk_a = at("rk_a", 205, [P, TT, ROPE // 2])
        rk_b = at("rk_b", 205.5, [P, TT, ROPE // 2])
        junk = at("junk", 199, [P, SEQ])
        trig = at("trig", 201, [P, 4, TT * ROPE // 2])
        invf = at("invf", 203, [P, ROPE // 2])
        pos_i = at("pos_i", 203.25, [P, TT], I32)
        pos_f = at("pos_f", 203.5, [P, TT])
        ln_g = at("ln_g", 148, [P, D])
        ln_b = at("ln_b", 156, [P, D])
        p_tok = at("p_tok", 164, [P, TT, PLE])
        pT = [at("pT_hi", 168, [P, PLE // P, SEQ], F32R), at("pT_lo", 172, [P, PLE // P, SEQ], F32R)]
        sig = at("sig", 176, [P, TT, BLK])
        pe_g = at("pe_g", 184, [P, TT, BLK])
        bstat = at("bstat", 205, [P, TT, NB, 6])
        bmean = at("bmean", 205.5, [P, TT, 2])
        rstd = at("rstd", 205.75, [P, TT])
        rvar = at("rvar", 205.875, [P, TT])
        FR = at("FR", 64, [P, 2, 2, 4, P])
        wst = at("wst", 72, [P, TT, 2, NH])
        EX = at("EX", 74, [P, 4, P])
        MM = at("MM", 76, [P, 4, P])
        CBU = at("CBU", 78, [P, P])
        CBL = at("CBL", 78.5, [P, P])
        st_b = at("st_b", 79, [P, 3, BLK])
        st_f = at("st_f", 85, [P, BLK])
        Xw = at("Xw", 87, [P, 2, BLK])
        uu = at("uu", 91, [P, BLK])
        Fs = at("Fs", 93, [P, TT, 2, NH])
        g_tot = at("g_tot", 95, [P, TT, 2, HG])
        g_d = at("g_d", 95.25, [P, HG])
        d_row = at("d_row", 145.71875, [P, NH])
        g_F = at("g_F", 147, [P, TT, 2, HG])
        g_dt = at("g_dt", 147.25, [P, TT, 2, HG])
        g_w = at("g_w", 147.5, [P, TT, 2, HG])
        g_e = at("g_e", 147.75, [P, TT, 2, HG])
        X = at("X", 148, [P, 2, TT, BLK])
        zs = at("zs", 164, [P, TT, BLK])
        BT = at("BT", 172, [P, 2, SEQ])
        CT = at("CT", 176, [P, 2, SEQ])
        Bt = at("Bt", 180, [P, 2, TT, NS])
        hp = at("hp", 184, [P, 4, SEQ + 2 * PAD])
        cv = at("cv", 192.25, [P, SEQ])
        eT = at("eT", 194.25, [P, TT, 2, NH])
        cw = at("cw", 196.25, [P, DI // P + 2 * NG, TAPS + 1])
        yg = at("yg", 197.75, [P, 2, BLK])
        yTc = at("yTc", 201.75, [P, 4, P])
        dt = at("dt", 203.75, [P, TT, 2, NH])
        eF = at("eF", 205.75, [P, TT, 2, NH])
        pre = [at(f"pre{i}", kb, [P, TT, 2 * NH]) for i, kb in enumerate((64, 66, 68, 70))]
        ones = at("ones", 76, [P, P])
        bias_row = at("bias_row", 78, [P, 2 * NH])
        alog_row = at("alog_row", 78.5, [P, 2 * NH])
        aa = at("aa", 80, [P, TT, 2 * NH])
        FT = at("FT", 82, [P, SEQ])
        yA = [at("yA_hi", 0, [P, KD, SEQ], F32R), at("yA_lo", 32, [P, KD, SEQ], F32R)]
        yB = [at("yB_hi", 148, [P, 12, SEQ], F32R), at("yB_lo", 172, [P, 12, SEQ], F32R)]
        yC = [at("yC_hi", 196, [P, 4, SEQ], F32R), at("yC_lo", 64, [P, TT, D], F32R)]
        yA_raw = at("yA_raw", 32, [P, KD, SEQ])
        yB_raw = at("yB_raw", 172, [P, 12, SEQ])
        yC_raw = at("yC_raw", 64, [P, TT, D])

        def y_part(i, k):
            if k < 16:
                return yA[i][:, k, :]
            if k < 28:
                return yB[i][:, k - 16, :]
            return yC[0][:, k - 28, :] if i == 0 else yC[1][:, k - 28, D - BLK:]

        def y_raw(k):
            return yA_raw[:, k, :] if k < 16 else yB_raw[:, k - 16, :] if k < 28 else yC_raw[:, k - 28, D - BLK:]

        def y_raw_quad(q):
            if q < 4:
                return yA_raw[:, 4 * q:4 * q + 4, :]
            return yB_raw[:, 4 * q - 16:4 * q - 12, :] if q < 7 else yC_raw[:, :, D - BLK:]

        g_cw = at("g_cw", 95.5, [P, GCH, TAPS + 1])
        ssq = stat[:, 64:64 + TT * NG].rearrange("p (c g) -> p c g", c=TT)
        x_mid = nc.dram_tensor("x_mid", (SEQ, D), F32, kind="Internal").ap()
        f_rows = nc.dram_tensor("f_rows", (2 * NH, SEQ), F32, kind="Internal").ap()
        y_scr = nc.dram_tensor("y_scr", (NG, P, 4, SEQ), F32, kind="Internal").ap()

        gemm = [ctx.enter_context(nc.psum_tensor(f"gemm{m}", [P, BLK], F32)) for m in range(4)]
        aux = [ctx.enter_context(nc.psum_tensor(f"aux{m}", [P, BLK], F32)) for m in range(4)]

        const_in = sem("const_in")
        x_in = [sem(f"x_in{t}") for t in range(TT)]
        raw_in = [sem(f"raw_in{s}") for s in range(2)]
        hi_done = sem("hi_done")
        split_done = sem("split_done")
        gemm_steps = sem("gemm_steps")
        aux_steps = sem("aux_steps")
        gemm_free = [sem(f"gemm_free{m}") for m in range(4)]
        aux_free = [sem(f"aux_free{m}") for m in range(4)]
        aux_hi = sem("aux_hi")
        aux_lo = sem("aux_lo")
        dve_order = sem("dve_order")
        pool_order = sem("pool_order")
        act_order = sem("act_order")
        ssq_done = sem("ssq_done")
        small_var = sem("small_var")
        small_std = sem("small_std")
        c_normed = sem("c_normed")
        trig_arg, trig_done = sem("trig_arg"), sem("trig_done")
        k_rotated = sem("k_rotated")
        q_rotated = sem("q_rotated")
        q_taken = sem("q_taken")
        qr_ready = sem("qr_ready")
        max_done, exp_done, norm_done, pt_done = sem("max_done"), sem("exp_done"), sem("norm_done"), sem("pt_done")
        g_split = sem("g_split")
        ln_in = sem("ln_in")
        resid = sem("resid")
        ln_stat, ln_scaled, ln_done = sem("ln_stat"), sem("ln_scaled"), sem("ln_done")
        sig_done, pe_done, x_done = sem("sig_done"), sem("pe_done"), sem("x_done")
        out_done = sem("out_done")
        p_in = sem("p_in")
        spill, ssd_const, alpha_done, resid1 = sem("spill"), sem("ssd_const"), sem("alpha_done"), sem("resid1")
        pad_zero = sem("pad_zero")
        dt_step = sem("dt_step")
        dt_act = sem("dt_act")
        ft_ready, ft_out = sem("ft_ready"), sem("ft_out")
        conv_done, silu_done = sem("conv_done"), sem("silu_done")
        fr_in = [sem("fr_in0"), sem("fr_in1")]
        group_scal = sem("group_scal")
        clipped = sem("clipped")
        summed = sem("summed")
        decayed = sem("decayed")
        weighted = sem("weighted")
        mixed_m = sem("mixed_m")
        xw_done = sem("xw_done")
        xd_done = sem("xd_done")
        state_done = sem("state_done")
        y_gated = sem("y_gated")
        y_squared = sem("y_squared")
        y_turned = sem("y_turned")
        y_out = sem("y_out")
        y_in = [sem(f"y_in{q}") for q in range(8)]
        y_hi, y_lo = sem("y_hi"), sem("y_lo")

        block = ctx.enter_context(nc.Block())

        def layer_norm_loads(sp, layer):
            if layer:
                sp.wait_ge(ln_stat, 2 * TT * NB)
            sp.dma_start(ln_g[:], lnw[2 * layer:2 * layer + 1, :].to_broadcast([P, D])).then_inc(ln_in, 16)
            sp.dma_start(ln_b[:], lnw[2 * layer + 1:2 * layer + 2, :].to_broadcast([P, D])).then_inc(ln_in, 16)
            sp.dma_start(p_tok[:], p[layer].rearrange("(t p) n -> p t n", p=P)).then_inc(p_in, 16)

        @block.sync
        def _(sp):
            unit = Count()

            def load_units(n):
                pairs, one = divmod(n - (unit.n % 2), 2)
                if unit.n % 2:
                    load_unit(unit.n)
                if pairs:
                    first = unit.n
                    if first == 0:
                        load_unit(0)
                        load_unit(1)
                        pairs -= 1
                    if pairs:
                        with turns(sp, pairs, [(unit, 2)]) as turn:
                            for s in range(2):
                                sp.wait_ge(split_done, unit.at(-1))
                                sp.dma_start(raw[:, s, :], wstream[bass.ds(unit.at(), 1), :, :]
                                             .rearrange("a p n -> p (a n)")).then_inc(raw_in[s], 16)
                                unit.step()
                if one:
                    load_unit(unit.n)

            def load_unit(u):
                if u >= 2:
                    sp.wait_ge(split_done, u - 1)
                sp.dma_start(raw[:, u % 2, :], wstream[u]).then_inc(raw_in[u % 2], 16)
                unit.step()

            for dst, n in ((ident, 0), (mask_le, 1), (mask_ge, 2)):
                sp.dma_start(dst[:], consts[n]).then_inc(const_in, 16)
            sp.dma_start(smalls[:], small).then_inc(const_in, 16)
            sp.dma_start(invf[:], rows[0:1, 0:ROPE // 2].to_broadcast([P, ROPE // 2])).then_inc(const_in, 16)
            sp.dma_start(pos_i[:], positions).then_inc(const_in, 16)
            for t in range(TT):
                sp.dma_start(xtok[:, t, :], x[t * P:(t + 1) * P, :]).then_inc(x_in[t], 16)
            load_units(U_CQ + U_CKV + U_KR + U_Z + U_ATT)
            load_units(4)
            sp.wait_ge(g_split, 4)
            sp.dma_start(xtok[:], x.rearrange("(t p) n -> p t n", p=P)).then_inc(resid, 16)
            layer_norm_loads(sp, 0)
            load_units(U_O - 4 + U_GATE + U_DT)
            load_units(2)
            load_units(NG * U_GRP - 2 + U_OUT + 2)
            layer_norm_loads(sp, 1)
            load_units(U_GATE)
            sp.wait_ge(x_done, 2 * TT * NB)
            sp.dma_start(out.rearrange("(t p) n -> p t n", p=P), xtok[:]).then_inc(out_done, 16)
            sp.wait_ge(out_done, 16)

        @block.tensor
        def _(pe):
            gfree = [Count() for _ in range(4)]
            afree = [Count() for _ in range(4)]
            units = Count()

            def passes(o, w, a, start, stop, swap=False):
                for n, (i, j) in enumerate(((0, 0), (0, 1), (1, 0))):
                    l, r = (a[j], w[i]) if swap else (w[i], a[j])
                    mm = pe.matmul(o, l, r, start=start and n == 0, stop=stop and n == 2)
                return mm

            def begin_unit():
                pe.wait_ge(split_done, units.step())

            def take_gemm(m):
                pe.wait_ge(gemm_free[m], gfree[m].at())
                gfree[m].step()

            def take_aux(m):
                pe.wait_ge(aux_free[m], afree[m].at())
                afree[m].step()

            def aux_read():
                for m in range(4):
                    pe.wait_ge(aux_free[m], afree[m].at())

            def product(*args, **kw):
                for _ in product_units(*args, **kw):
                    pass

            def product_units(acts, k_tiles, tokens_out, banks=None, take=take_gemm, order=None):
                ku = UNIT // BLK
                first = order[0] if order else 0
                last = (order[-1] if order else (k_tiles - 1) // ku * ku) + min(ku, k_tiles) - 1
                if isinstance(acts, list):
                    acts = (lambda parts: lambda i, k: parts[i][:, k, :])(acts)
                for k0 in order or range(0, k_tiles, ku):
                    slot = units.n % 2
                    begin_unit()
                    kn = min(ku, k_tiles - k0)
                    for m in range(4):
                        if k0 == first:
                            take(m)
                        for k in range(kn):
                            sl = slice(k * BLK, (k + 1) * BLK) if tokens_out else slice(k * BLK + m * P, k * BLK + (m + 1) * P)
                            w = [W[i][:, slot, sl] for i in range(2)]
                            a = [acts(i, k0 + k)[:, m * P:(m + 1) * P] if tokens_out else acts(i, k0 + k) for i in range(2)]
                            mm = passes((banks or gemm)[m][:], w, a, k0 + k == first, k0 + k == last, swap=tokens_out)
                        mm.then_inc(gemm_steps, 1)
                    yield

            def transpose_tokens():
                for t in range(TT):
                    yield t
                    for b in range(4):
                        take_aux(b)
                        for k in range(4):
                            f = 4 * b + k
                            tr = pe.transpose(aux[b][:, k * P:(k + 1) * P], xtok[:, t, f * P:(f + 1) * P], ident[:])
                        tr.then_inc(aux_steps, 1)

            pe.wait_ge(const_in, 16 * 6)
            for t in transpose_tokens():
                pe.wait_ge(x_in[t], 16)
            aux_read()
            product(xT, KD, True)
            product(xT, KD, True)
            slot = units.n % 2
            begin_unit()
            for m in range(4):
                take_gemm(m)
                for k in range(KD):
                    w = [W[i][:, slot, k * ROPE:(k + 1) * ROPE] for i in range(2)]
                    a = [xT[i][:, k, m * P:(m + 1) * P] for i in range(2)]
                    mm = passes(gemm[m][:, 0:ROPE], w, a, k == 0, k == KD - 1, swap=True)
                mm.then_inc(gemm_steps, 1)
            with turns(pe, NB, [(c, 1) for c in gfree] + [(units, 4)]):
                product(xT, KD, False)
            pe.wait_ge(c_normed, 2 * TT)
            for f in range(2 * KL):
                take_aux(f % 4)
                for t in range(TT):
                    tr = pe.transpose(aux[f % 4][:, t * P:(t + 1) * P],
                                      c_tok[:, f // KL, t, (f % KL) * P:(f % KL + 1) * P], ident[:])
                tr.then_inc(aux_steps, 1)
            pe.wait_ge(k_rotated, 2)
            take_aux(0)
            for t in range(TT):
                tr = pe.transpose(aux[0][:, t * P:(t + 1) * P], k_rot[:, t].rearrange("p a b -> p (a b)"), ident[:])
            tr.then_inc(aux_steps, 1)
            aux_read()

            norm_seen, q_seen = Count(), Count()

            def qkv(pair_slot):
                slot = units.n % 2
                begin_unit()
                wq = [W[i][:, slot, 0:KL * 2 * QKH].rearrange("p (k h n) -> p k h n", k=KL, h=2) for i in range(2)]
                for h in range(2):
                    take_gemm(h)
                    for k in range(KL):
                        mm = passes(gemm[h][:], [w[:, k, h, 0:NOPE] for w in wq], [c[:, k, :] for c in cT],
                                    k == 0, k == KL - 1)
                    mm.then_inc(gemm_steps, 1)
                take_gemm(2)
                for t in range(TT):
                    for k in range(KL):
                        mm = passes(gemm[2][:, t * 2 * ROPE:(t + 1) * 2 * ROPE], [w[:, k, :, NOPE:QKH] for w in wq],
                                    [c[:, k, t * P:(t + 1) * P] for c in cT], k == 0, k == KL - 1, swap=True)
                    if t % 2:
                        mm.then_inc(gemm_steps, 1)
                slot = units.n % 2
                begin_unit()
                wk = [W[i][:, slot, :].rearrange("p (k h n) -> p k h n", k=KL, h=2) for i in range(2)]
                for h, m in ((0, 3), (1, 0)):
                    take_gemm(m)
                    for k in range(KL):
                        mm = passes(gemm[m][:], [w[:, k, h, 0:NOPE] for w in wk], [c[:, KL + k, :] for c in cT],
                                    k == 0, k == KL - 1)
                    mm.then_inc(gemm_steps, 1)
                for m in (1, 2):
                    take_gemm(m)
                    for j in range(2):
                        t = 2 * (m - 1) + j
                        for k in range(KL):
                            mm = passes(gemm[m][:, j * 2 * VH:(j + 1) * 2 * VH], [w[:, k, :, NOPE:] for w in wk],
                                        [c[:, KL + k, t * P:(t + 1) * P] for c in cT], k == 0, k == KL - 1, swap=True)
                    mm.then_inc(gemm_steps, 1)

            def attend(s):
                pe.wait_ge(q_rotated, q_seen.step())
                take_aux(3)
                for t in range(TT):
                    tr = pe.transpose(aux[3][:, t * P:(t + 1) * P], q_rot[:, t].rearrange("p h a b -> p (h a b)"), ident[:])
                tr.then_inc(aux_steps, 1)
                pe.wait_ge(aux_free[3], afree[3].at())

                def scores(n):
                    h, t = divmod(n, TT)
                    pe.matmul(aux[n % 2][:], qT[:, s, h, t * P:(t + 1) * P], kT[:, s, h, :], start=True, stop=False)
                    pe.matmul(aux[n % 2][:], qrT[h * ROPE:(h + 1) * ROPE, s, t * P:(t + 1) * P],
                              krT[h * ROPE:(h + 1) * ROPE, :], start=False, stop=True).then_inc(aux_steps, 1)

                def turn_probs(n):
                    pe.wait_ge(norm_done, norm_seen.step())
                    take_aux(2 + n % 2)
                    for k in range(TT):
                        tr = pe.transpose(aux[2 + n % 2][:, k * P:(k + 1) * P], prob[:, n % 2, k * P:(k + 1) * P], ident[:])
                    tr.then_inc(aux_steps, 1)

                def values(h):
                    pe.wait_ge(aux_free[2], afree[2].at())
                    pe.wait_ge(aux_free[3], afree[3].at())
                    take_aux(2)
                    for k in range(TT):
                        mm = pe.matmul(aux[2][:], v_tok[:, s, k, h * VH:(h + 1) * VH], PT[:, h, k, :],
                                       start=k == 0, stop=k == TT - 1)
                    mm.then_inc(aux_steps, 1)

                scores(0)
                scores(1)
                for n in range(2 * TT):
                    turn_probs(n)
                    if n + 2 < 2 * TT:
                        scores(n + 2)
                    if n == TT:
                        values(0)
                values(1)

            qkv(0)
            loop = ([(gfree[0], 4), (gfree[1], 4), (gfree[2], 4), (gfree[3], 2), (units, 4)]
                    + [(afree[2], 12), (afree[3], 10), (q_seen, 2), (norm_seen, 16)])
            with turns(pe, PAIRS // 2 - 1, loop):
                for s in range(2):
                    qkv(1 - s)
                    attend(s)
            qkv(1)
            attend(0)
            attend(1)

            pe.wait_ge(g_split, 4)
            with turns(pe, NB, [(c, 1) for c in gfree] + [(units, 4)]):
                product(xT, KD, True)

            def norm_and_gate(layer):
                pe.wait_ge(p_in, 16 * (layer + 1))
                for f in range(PLE // P):
                    take_aux(f)
                    for t in range(TT):
                        tr = pe.transpose(aux[f][:, t * P:(t + 1) * P], p_tok[:, t, f * P:(f + 1) * P], ident[:])
                    tr.then_inc(aux_steps, 1)
                for t in transpose_tokens():
                    pe.wait_ge(ln_done, layer * TT + t + 1)
                aux_read()
                with turns(pe, NB // 2, [(c, 2) for c in gfree + afree] + [(units, 10)]):
                    for _ in range(2):
                        product(pT, PLE // P, True, banks=aux, take=take_aux)
                        product(xT, KD, True)

            norm_and_gate(0)

            for t in transpose_tokens():
                pe.wait_ge(x_done, TT * NB)
            aux_read()
            slot = units.n % 2
            begin_unit()
            for m in range(4):
                take_gemm(m)
                for k in range(KD):
                    mm = passes(gemm[m][:, 0:2 * NH], [w[:, slot, k * 2 * NH:(k + 1) * 2 * NH] for w in W],
                                [x[:, k, m * P:(m + 1) * P] for x in xT], k == 0, k == KD - 1, swap=True)
                mm.then_inc(gemm_steps, 1)
            pe.wait_ge(dt_step, 2)
            pe.wait_ge(ssd_const, 16 * 5)
            take_aux(0)
            for c in range(TT):
                for d, tri in enumerate((mask_le, mask_ge)):
                    o = c * 2 * NH + d * NH
                    mm = pe.matmul(aux[0][:, o:o + NH], tri[:], aa[:, c, d * NH:(d + 1) * NH], start=True, stop=True)
            mm.then_inc(aux_steps, 1)
            take_aux(1)
            mm = pe.matmul(aux[1][:], ones[:], aa[:].rearrange("p c n -> p (c n)"), start=True, stop=True)
            mm.then_inc(aux_steps, 1)
            pe.wait_ge(dt_step, 3)
            take_aux(2)
            for c in range(TT):
                tr = pe.transpose(aux[2][:, c * P:(c + 1) * P], Fs[:, c].rearrange("p d h -> p (d h)"), ident[:])
            tr.then_inc(aux_steps, 1)

            silu, mixed_n, xw, gated = Count(), Count(), Count(), Count()

            def extras(j, fills, s):
                o = 1 - s
                if j == 0 and any(n[0] == "cb" for _, n, _ in fills):
                    pe.wait_ge(silu_done, silu.at())
                    aux_read()
                for slot_j, (what, n), bank in fills:
                    if slot_j != j:
                        continue
                    if what != "intra" or n % 2 == 0:
                        take_aux(bank)
                    b = aux[bank]
                    if what == "intra":
                        pe.wait_ge(mixed_m, mixed_n.step())
                        c, hf = divmod(n, 2)
                        for h in range(4):
                            cols = slice((4 * hf + h) * HD, (4 * hf + h + 1) * HD)
                            mm = pe.matmul(b[:, cols], MM[:, h, :], X[:, o, c, cols], start=True, stop=True)
                    elif what == "cb":
                        mm = pe.matmul(b[:, 0:P], BT[:, o, n * P:(n + 1) * P], CT[:, o, n * P:(n + 1) * P], start=True, stop=True)
                    elif what in ("back", "forth"):
                        pe.wait_ge(xw_done, xw.step())
                        buf = {("back", 3): 0, ("back", 2): 1, ("back", 1): 0}.get((what, n), n % 2)
                        mm = pe.matmul(b[:], Bt[:, o, n, :], Xw[:, buf, :], start=True, stop=True)
                    elif what == "from_f":
                        mm = pe.matmul(b[:], CT[:, o, n * P:(n + 1) * P], st_f[:], start=True, stop=True)
                    elif what == "from_b":
                        if n == 0:
                            pe.wait_ge(aux_free[1], afree[1].at())
                        mm = pe.matmul(b[:], CT[:, o, n * P:(n + 1) * P], st_b[:, n, :], start=True, stop=True)
                    elif what == "ytr":
                        pe.wait_ge(y_gated, gated.step())
                        for f in range(4):
                            mm = pe.transpose(b[:, f * P:(f + 1) * P], yg[:, n % 2, f * P:(f + 1) * P], ident[:])
                    else:
                        pe.wait_ge(silu_done, silu.at(n + 1))
                        src = cv[:] if n < 4 else BT[:, s, :]
                        for t in range(TT):
                            mm = pe.transpose(b[:, t * P:(t + 1) * P], src[:, t * P:(t + 1) * P], ident[:])
                    mm.then_inc(aux_steps, 1)

            def group(s, products, ssd):
                fills = group_fills(products, ssd)
                if products:
                    j = 0
                    for _ in product_units(xT, KD, False):
                        extras(j, fills, s)
                        j += 1
                    for half in range(2):
                        slot = units.n % 2
                        begin_unit()
                        for i, m in enumerate((2, 3)):
                            if half == 0:
                                take_gemm(m)
                            for k in range(8):
                                kk = 8 * half + k
                                o = k * 2 * NS + i * NS
                                mm = passes(gemm[m][:], [w[:, slot, o:o + NS] for w in W], [x[:, kk, :] for x in xT],
                                            kk == 0, kk == KD - 1)
                                if k % 4 == 3:
                                    mm.then_inc(gemm_steps, 1)
                        extras(j, fills, s)
                        j += 1
                    for _ in product_units(xT, KD, True):
                        extras(j, fills, s)
                        j += 1
                    silu.step(GCH)
                else:
                    for j in range(U_GRP):
                        extras(j, fills, s)
            group(0, True, False)
            both = group_fills(True, True)
            per = [2 * bank_count(both, m) for m in range(4)]
            with turns(pe, NG // 2 - 1, [(c, n) for c, n in zip(afree, per)] + [(gfree[0], 4), (gfree[1], 4), (gfree[2], 6),
                       (gfree[3], 6), (units, 2 * U_GRP), (silu, 2 * GCH), (mixed_n, 16), (xw, 12), (gated, 8)]):
                group(1, True, True)
                group(0, True, True)
            group(1, True, True)
            group(0, False, True)

            pe.wait_ge(y_lo, 32)
            with turns(pe, NB, [(c, 1) for c in gfree] + [(units, 8)]):
                product(y_part, 2 * KD, True, order=[28, 0, 4, 8, 12, 16, 20, 24])
            norm_and_gate(1)

        @block.scalar
        def _(act):
            split_unit = Count()
            step0 = Count()
            aux0 = Count()
            order = Count()

            def split():
                s = split_unit.n % 2
                act.wait_ge(gemm_steps, step0.at())
                act.wait_ge(raw_in[s], slot_uses(split_unit))
                act.activation(W[0][:, s, :], raw[:, s, :], ACT.Copy).then_inc(hi_done, 1)
                split_unit.step()

            def next_unit():
                step0.step(4)
                split()

            def split_aux_tokens(t, b):
                act.wait_ge(aux_steps, aux0.step())
                act.activation(xT[0][:, 4 * b:4 * b + 4, t * P:(t + 1) * P],
                               aux[b][:].rearrange("p (k n) -> p k n", k=4), ACT.Copy).then_inc(aux_hi, 1)

            split()
            split()
            for t in range(TT):
                for b in range(4):
                    split_aux_tokens(t, b)
            for j in range(2):
                for u in range(4):
                    next_unit()
                for t in range(TT):
                    act.wait_ge(gemm_free[t], j + 1)
                    if j or t:
                        act.wait_ge(ssq_done, j * TT + t)
                    act.activation(junk[:], c_tok[:, j, t, :], ACT.Square,
                                   accum_out=stat[:, j * TT + t:j * TT + t + 1]).then_inc(ssq_done, 1)
            next_unit()
            act.wait_ge(small_var, 1)
            act.activation(stat[:, 16:24], stat[:, 8:16], ACT.Sqrt).then_inc(small_std, 1)
            act.wait_ge(trig_arg, 2)
            act.activation(sin[:].rearrange("p t n -> p (t n)"), trig[:, 0, :], ACT.Sin).then_inc(trig_done, 1)
            act.activation(cos[:].rearrange("p t n -> p (t n)"), trig[:, 1, :], ACT.Sin).then_inc(trig_done, 1)
            with turns(act, NB, [(split_unit, 4), (step0, 16)]) as turn:
                for u in range(4):
                    if u == 3:
                        for m in range(4):
                            act.wait_ge(gemm_steps, step0.at(m + 1))
                            act.activation(zT[:, bass.ds(turn * 4 + m, 1), :].rearrange("p a n -> p (a n)"),
                                           gemm[m][:], ACT.Silu).then_inc(gemm_free[m], 1)
                    next_unit()
            for f in range(2 * KL):
                act.wait_ge(aux_steps, aux0.step())
                act.activation(cT[0][:, f, :], aux[f % 4][:], ACT.Copy, scale=smalls[:, f:f + 1]).then_inc(aux_hi, 1)
            aux0.step()

            maxes, pts, norms = Count(), Count(), Count()

            def take_qkv(s):
                for h in range(2):
                    act.wait_ge(gemm_steps, step0.at(h + 1))
                    act.activation(qT[:, s, h, :], gemm[h][:], ACT.Copy).then_inc(gemm_free[h], 1)
                next_unit()
                act.wait_ge(gemm_steps, step0.at(2))
                act.activation(kT[:, s, 1, :], gemm[0][:], ACT.Copy).then_inc(gemm_free[0], 1)
                act.wait_ge(gemm_steps, step0.at(4))
                act.activation(v_tok[:, s, 2:4, :].rearrange("p t n -> p (t n)"), gemm[2][:], ACT.Copy).then_inc(gemm_free[2], 1)
                next_unit()

            def attend(s):
                aux0.step()
                a = {"S": [1, 2, 4, 6, 8, 10, 12, 15], "T": [3, 5, 7, 9, 11, 14, 16, 17]}

                def exp(n):
                    act.wait_ge(max_done, maxes.step())
                    act.wait_ge(aux_steps, aux0.at(a["S"][n]))
                    act.wait_ge(aux_steps, aux0.at(a["T"][n - 2] if n >= 2 else 0))
                    act.activation(prob[:, n % 2, :], aux[n % 2][:], ACT.Exp, bias=stat[:, 40 + n:41 + n], scale=SCALE,
                                   accum_out=stat[:, 48 + n:49 + n]).then_inc(exp_done, 1)

                def take_pt(n):
                    h, t = divmod(n, TT)
                    act.wait_ge(aux_steps, aux0.at(a["T"][n]))
                    act.activation(PT[:, h, :, t * P:(t + 1) * P], aux[2 + n % 2][:].rearrange("p (k n) -> p k n", k=TT),
                                   ACT.Copy).then_inc(aux_free[2 + n % 2], 1)
                    pts.step()

                exp(0)
                exp(1)
                for n in range(2 * TT):
                    take_pt(n)
                    if n + 2 < 2 * TT:
                        exp(n + 2)
                aux0.step(18)

            take_qkv(0)
            with turns(act, PAIRS // 2 - 1, [(split_unit, 4), (step0, 16), (aux0, 38), (maxes, 16), (pts, 16)]):
                for s in range(2):
                    take_qkv(1 - s)
                    attend(s)
            take_qkv(1)
            attend(0)
            attend(1)

            act.wait_ge(aux_free[2], AUX2_ATT)
            for q in range(4):
                act.activation(xT[0][:, 4 * q:4 * q + 4, :].rearrange("p k n -> p (k n)"),
                               g_raw[:, 4 * q:4 * q + 4, :].rearrange("p k n -> p (k n)"), ACT.Copy).then_inc(aux_hi, 1)
            with turns(act, NB, [(split_unit, 4), (step0, 16)]):
                for u in range(4):
                    next_unit()

            def norm_and_gate(layer):
                for f in range(PLE // P):
                    act.wait_ge(aux_steps, aux0.step())
                    act.activation(pT[0][:, f, :], aux[f][:], ACT.Copy).then_inc(aux_hi, 1)
                act.wait_ge(small_var, 2 + 2 * layer)
                act.activation(rstd[:], rvar[:], ACT.Sqrt).then_inc(small_std, 1)
                for t in range(TT):
                    for b in range(4):
                        split_aux_tokens(t, b)
                with turns(act, NB // 2, [(split_unit, 10), (step0, 40)]):
                    for cb in range(2):
                        for u in range(5):
                            if u == 4:
                                for t in range(TT):
                                    act.wait_ge(gemm_steps, step0.at(t + 1))
                                    act.activation(sig[:, t, :], gemm[t][:], ACT.Sigmoid).then_inc(gemm_free[t], 1)
                            next_unit()

            norm_and_gate(0)

            act.wait_ge(x_done, TT * NB)
            act.dma_start(x_mid.rearrange("(t p) n -> p t n", p=P), xtok[:]).then_inc(spill, 16)
            for t in range(TT):
                for b in range(4):
                    split_aux_tokens(t, b)
            act.wait_ge(spill, 16)
            act.wait_ge(pad_zero, 1)
            act.dma_start(ones[:], consts[3]).then_inc(ssd_const, 16)
            act.dma_start(bias_row[:], rows[0:1, 32:160].to_broadcast([P, 2 * NH])).then_inc(ssd_const, 16)
            act.dma_start(alog_row[:], rows[0:1, 160:288].to_broadcast([P, 2 * NH])).then_inc(ssd_const, 16)
            act.dma_start(d_row[:], rows[0:1, 288:352].to_broadcast([P, NH])).then_inc(ssd_const, 16)
            act.dma_start(cw[:], convw).then_inc(ssd_const, 16)
            next_unit()
            act.wait_ge(ssd_const, 16 * 5)
            act.activation(alog_row[:], alog_row[:], ACT.Exp).then_inc(dt_act, 1)
            act.wait_ge(dt_step, 1)
            act.activation(pre[1][:], pre[1][:], ACT.Exp, scale=-1.0).then_inc(dt_act, 1)
            flat = lambda v: v[:].rearrange("p t d h -> p (t d h)")
            act.wait_ge(dt_step, 3)
            act.activation(flat(eF), flat(Fs), ACT.Exp).then_inc(dt_act, 1)
            act.activation(flat(wst), flat(wst), ACT.Exp).then_inc(dt_act, 1)
            act.activation(flat(eT), flat(eT), ACT.Exp).then_inc(dt_act, 1)
            act.wait_ge(aux_free[2], AUX2_ATT + 2 * TT + NB + 1)
            act.dma_start(f_rows, FT[:]).then_inc(ft_out, 16)
            act.wait_ge(ft_out, 16)
            aux0.step(3)
            sums, convs, gates, outs = [Count() for _ in range(4)]

            def rows_of(q, g):
                c, hf = divmod(q, 2)
                for d in range(2):
                    src = f_rows[bass.ds(g * HG + d * NH + 4 * hf, 4), c * P:(c + 1) * P].unsqueeze(0).to_broadcast([P, 4, P])
                    act.dma_start(FR[:, q % 2, d], src).then_inc(fr_in[q % 2], 16)

            def group(s, g, products, ssd):
                fills = group_fills(products, ssd)
                o = 1 - s
                for j in range(U_GRP):
                    if products:
                        if j == 3:
                            for m in range(4):
                                act.wait_ge(gemm_steps, step0.at(m + 1))
                                act.wait_ge(conv_done, convs.at())
                                act.activation(hp[:, m, PAD:PAD + SEQ], gemm[m][:], ACT.Copy).then_inc(gemm_free[m], 1)
                        if j == 5:
                            act.wait_ge(gemm_steps, step0.at(2))
                            act.wait_ge(conv_done, convs.at(1))
                            act.activation(hp[:, 0, PAD:PAD + SEQ], gemm[2][:], ACT.Copy).then_inc(gemm_free[2], 1)
                        if j == 9:
                            if ssd:
                                act.wait_ge(y_gated, gates.at(1))
                            for t in range(TT):
                                act.wait_ge(gemm_steps, step0.at(t + 1))
                                act.activation(zs[:, t, :], gemm[t][:], ACT.Silu).then_inc(gemm_free[t], 1)
                        next_unit()
                    if ssd:
                        if j == 0:
                            rows_of(0, g - 1)
                            rows_of(1, g - 1)
                        if j < 8:
                            act.wait_ge(summed, sums.step())
                            act.activation(EX[:], EX[:], ACT.Exp).then_inc(decayed, 1)
                        if j < 6:
                            rows_of(j + 2, g - 1)
                        if j in (3, 5, 7, 9):
                            c = (j - 3) // 2
                            act.wait_ge(y_gated, gates.step())
                            act.wait_ge(aux_steps, aux0.at(fill_no(fills, ("ytr", c))))
                            act.wait_ge(y_out, outs.at())
                            act.activation(yTc[:].rearrange("p f n -> p (f n)"), yg[:, c % 2, :], ACT.Square,
                                           accum_out=ssq[:, c, bass.ds(g - 1, 1)]).then_inc(y_squared, 1)
                            act.wait_ge(y_squared, gates.at())
                            act.activation(yTc[:].rearrange("p f n -> p (f n)"), aux[0][:], ACT.Copy).then_inc(aux_free[0], 1)
                            act.wait_ge(aux_free[0], free0.at(bank_no(fills, ("ytr", c))))
                            act.dma_start(y_scr[bass.ds(g - 1, 1), :, :, c * P:(c + 1) * P].rearrange("a p f n -> p (a f) n"),
                                          yTc[:]).then_inc(y_out, 16)
                            outs.step(16)
                    if products and j >= 4:
                        n = j - 4
                        if n >= 1:
                            act.wait_ge(aux_steps, aux0.at(fill_no(fills, ("ctr", n - 1))))
                            bank = 2 if j % 2 else 0
                            dst = X[:, s, :, (n - 1) * P:n * P] if n <= 4 else Bt[:, s]
                            act.activation(dst, aux[bank][:].rearrange("p (t n) -> p t n", t=TT), ACT.Copy)\
                               .then_inc(aux_free[bank], 1)
                        act.wait_ge(conv_done, convs.at(n + 1))
                        dst = cv[:] if n < 4 else (BT if n == 4 else CT)[:, s, :]
                        act.activation(dst, cv[:], ACT.Silu).then_inc(silu_done, 1)
                        if j == 5:
                            act.wait_ge(gemm_steps, step0.at(0))
                            act.activation(hp[:, 1, PAD:PAD + SEQ], gemm[3][:], ACT.Copy).then_inc(gemm_free[3], 1)
                if products:
                    convs.step(GCH)
                aux0.step(len(fills))
                free0.step(bank_count(fills, 0))

            free0 = Count(AUX0_SSD)
            group(0, 0, True, False)
            both = group_fills(True, True)
            with turns(act, NG // 2 - 1, [(split_unit, 2 * U_GRP), (step0, 8 * U_GRP), (aux0, 2 * len(both)),
                       (free0, 2 * bank_count(both, 0)), (convs, 2 * GCH), (sums, 16), (gates, 8), (outs, 128)]) as turn:
                group(1, turn * 2 + 1, True, True)
                group(0, turn * 2 + 2, True, True)
            group(1, NG - 1, True, True)
            group(0, NG, False, True)

            act.wait_ge(y_out, outs.at())
            for q in (7, 0, 1, 2, 3, 4, 5, 6):
                dst = y_raw_quad(q)
                act.dma_start(dst, y_scr[q]).then_inc(y_in[q], 16)
            act.dma_start(xtok[:, :, 0:D - BLK], x_mid.rearrange("(t p) n -> p t n", p=P)[:, :, 0:D - BLK]).then_inc(resid1, 16)
            act.wait_ge(small_var, 3)
            act.activation(stat[:, 104:108], stat[:, 100:104], ACT.Sqrt).then_inc(small_std, 1)
            for q in (7, 0, 1, 2, 3, 4, 5, 6):
                act.wait_ge(y_in[q], 16)
                for k in range(4 * q, 4 * q + 4):
                    act.activation(y_part(0, k), y_raw(k), ACT.Copy, scale=smalls[:, 8 + k:9 + k]).then_inc(y_hi, 1)
            with turns(act, NB - 1, [(split_unit, 8), (step0, 32)]):
                for u in range(8):
                    next_unit()
            for u in range(8):
                next_unit()
                if u == 0:
                    act.dma_start(xtok[:, :, D - BLK:], x_mid.rearrange("(t p) n -> p t n", p=P)[:, :, D - BLK:]).then_inc(resid1, 16)
            norm_and_gate(1)

        @block.vector
        def _(dve):
            split_unit, step0, aux0, hi = Count(), Count(), Count(), Count()
            gfree = [Count() for _ in range(4)]
            afree = [Count() for _ in range(4)]
            order, gfull = Count(), Count()

            def link(ins):
                ins.then_inc(dve_order, 1)
                dve.wait_ge(dve_order, order.step())

            def split():
                s = split_unit.n % 2
                dve.wait_ge(hi_done, split_unit.at(1))
                dve.tensor_tensor(W[1][:, s, :], raw[:, s, :], W[0][:, s, :].bitcast(F32), ALU.subtract)\
                   .then_inc(split_done, 1)
                split_unit.step()

            def next_unit():
                step0.step(4)
                split()

            def freed(ins, which, counts, m):
                ins.then_inc(which[m], 1)
                counts[m].step()

            def split_aux_tokens(t, b):
                aux0.step()
                dve.wait_ge(aux_hi, hi.step())
                dst = slice(t * P, (t + 1) * P)
                freed(dve.tensor_tensor(xT[1][:, 4 * b:4 * b + 4, dst], aux[b][:].rearrange("p (k n) -> p k n", k=4),
                                        xT[0][:, 4 * b:4 * b + 4, dst].bitcast(F32), ALU.subtract), aux_free, afree, b)

            dve.wait_ge(const_in, 16 * 6)
            link(dve.tensor_copy(pos_f[:], pos_i[:]))
            for t in range(TT):
                ins = dve.tensor_scalar(trig[:, 2, t * 32:(t + 1) * 32], invf[:], pos_f[:, t:t + 1], None, ALU.mult)
            link(ins)
            for n, quarter in enumerate((0.0, 0.25)):
                k, r = trig[:, 3, :], trig[:, n, :]
                link(dve.tensor_scalar(k, trig[:, 2, :], float(1 / (2 * np.pi)), quarter, ALU.mult, ALU.add))
                link(dve.tensor_scalar(k, k, ROUND, None, ALU.add))
                link(dve.tensor_scalar(k, k, -ROUND, None, ALU.add))
                link(dve.scalar_tensor_tensor(r, k, -TWO_PI_PARTS[0], trig[:, 2, :], ALU.mult, ALU.add))
                link(dve.scalar_tensor_tensor(r, k, -TWO_PI_PARTS[1], r, ALU.mult, ALU.add))
                link(dve.scalar_tensor_tensor(r, k, -TWO_PI_PARTS[2], r, ALU.mult, ALU.add))
                link(dve.tensor_scalar(r, r, float(2 * np.pi * quarter), PI32, ALU.add, ALU.min))
                dve.tensor_scalar(r, r, -PI32, None, ALU.max).then_inc(trig_arg, 1)

            split()
            split()
            for t in range(TT):
                for b in range(4):
                    split_aux_tokens(t, b)
            for j in range(2):
                for u in range(4):
                    if u == 3:
                        for t in range(TT):
                            dve.wait_ge(gemm_steps, step0.at(t + 1))
                            freed(dve.tensor_copy(c_tok[:, j, t, :], gemm[t][:]), gemm_free, gfree, t)
                    next_unit()
            for t in range(TT):
                dve.wait_ge(gemm_steps, step0.at(t + 1))
                freed(dve.tensor_copy(k_tok[:, t, :], gemm[t][:, 0:ROPE]), gemm_free, gfree, t)
            next_unit()
            dve.wait_ge(ssq_done, 2 * TT)
            dve.tensor_scalar(stat[:, 8:16], stat[:, 0:8], 1.0 / LORA, RMS_EPS, ALU.mult, ALU.add).then_inc(small_var, 1)
            dve.wait_ge(small_std, 1)
            link(dve.reciprocal(stat[:, 24:32], stat[:, 16:24]))
            for j in range(2):
                for t in range(TT):
                    dve.tensor_scalar(c_tok[:, j, t, :], c_tok[:, j, t, :], stat[:, 24 + j * TT + t:25 + j * TT + t],
                                      None, ALU.mult).then_inc(c_normed, 1)
            with turns(dve, NB, [(split_unit, 4), (step0, 16)] + [(c, 1) for c in gfree]):
                for u in range(4):
                    next_unit()
                for c in gfree:
                    c.step()
            for f in range(2 * KL):
                aux0.step()
                dve.wait_ge(aux_hi, hi.step())
                freed(dve.scalar_tensor_tensor(cT[1][:, f, :], aux[f % 4][:], smalls[:, f:f + 1],
                                               cT[0][:, f, :].bitcast(F32), ALU.mult, ALU.subtract), aux_free, afree, f % 4)
            dve.wait_ge(aux_steps, aux0.step())
            freed(dve.tensor_copy(krT[:], aux[0][:]), aux_free, afree, 0)

            exps = Count()

            def take_qkv(s):
                dve.wait_ge(gemm_steps, step0.at(4))
                dve.wait_ge(q_rotated, pairs.at())
                dve.tensor_copy(q_tok[:].rearrange("p t h a b -> p (t h a b)"), gemm[2][:]).then_inc(gemm_free[2], 1)
                pairs.step()
                next_unit()
                dve.wait_ge(gemm_steps, step0.at(1))
                dve.tensor_copy(kT[:, s, 0, :], gemm[3][:]).then_inc(gemm_free[3], 1)
                dve.wait_ge(gemm_steps, step0.at(3))
                dve.tensor_copy(v_tok[:, s, 0:2, :].rearrange("p t n -> p (t n)"), gemm[1][:]).then_inc(gemm_free[1], 1)
                next_unit()
                gfree[0].step(2), gfree[1].step(2), gfree[2].step(2), gfree[3].step(1)

            pairs = Count()

            def attend(s, pair):
                dve.wait_ge(aux_steps, aux0.step())
                dve.tensor_copy(qrT[:, s, :], aux[3][:]).then_inc(aux_free[3], 1)
                a_s = [1, 2, 4, 6, 8, 10, 12, 15]

                def top(n):
                    dve.wait_ge(aux_steps, aux0.at(a_s[n]))
                    link(dve.tensor_reduce(stat[:, 32 + n:33 + n], aux[n % 2][:], AX.X, ALU.max))
                    dve.tensor_scalar(stat[:, 40 + n:41 + n], stat[:, 32 + n:33 + n], -SCALE, None, ALU.mult).then_inc(max_done, 1)

                def normalise(n):
                    dve.wait_ge(exp_done, exps.step())
                    link(dve.reciprocal(stat[:, 56 + n:57 + n], stat[:, 48 + n:49 + n]))
                    dve.tensor_scalar(prob[:, n % 2, :], prob[:, n % 2, :], stat[:, 56 + n:57 + n], None,
                                      ALU.mult).then_inc(norm_done, 1)

                def gate(h, fill):
                    dve.wait_ge(aux_steps, aux0.at(fill))
                    g = (pair * 2 + h)
                    dve.tensor_tensor(g_raw[:, bass.ds(g, 1), :].rearrange("p a n -> p (a n)"), aux[2][:],
                                      zT[:, bass.ds(g, 1), :].rearrange("p a n -> p (a n)"), ALU.mult).then_inc(aux_free[2], 1)

                top(0)
                top(1)
                for n in range(2 * TT):
                    normalise(n)
                    if n + 2 < 2 * TT:
                        top(n + 2)
                    if n == 5:
                        gate(0, 13)
                gate(1, 18)
                aux0.step(18)
                afree[2].step(6), afree[3].step(5)

            take_qkv(0)
            with turns(dve, PAIRS // 2 - 1, [(split_unit, 4), (step0, 16), (aux0, 38), (order, 32), (exps, 16), (pairs, 2)]
                       + [(gfree[0], 4), (gfree[1], 4), (gfree[2], 4), (gfree[3], 2), (afree[2], 12), (afree[3], 10)]) as turn:
                for s in range(2):
                    take_qkv(1 - s)
                    attend(s, turn * 2 + s)
            take_qkv(1)
            attend(0, PAIRS - 2)
            attend(1, PAIRS - 1)

            for q in range(4):
                dve.wait_ge(aux_hi, hi.step())
                a = slice(4 * q, 4 * q + 4)
                dve.tensor_tensor(xT[1][:, a, :], g_raw[:, a, :], xT[0][:, a, :].bitcast(F32), ALU.subtract).then_inc(g_split, 1)

            def mixed(layer, n_blocks, first, units_of_block):
                def block(cb):
                    for u in range(units_of_block):
                        if u == units_of_block - 1:
                            for t in range(TT):
                                xb = xtok[:, t, bass.ds(cb * BLK, BLK)]
                                dve.wait_ge(gemm_steps, step0.at(t + 1))
                                if layer == 0:
                                    ins = dve.scalar_tensor_tensor(xb, xb, ALPHA, gemm[t][:], ALU.mult, ALU.add)
                                else:
                                    ins = dve.scalar_tensor_tensor(xb, gemm[t][:], stat[:, 108 + t:109 + t], xb, ALU.mult, ALU.add)
                                freed(ins, gemm_free, gfree, t)
                                dve.wait_ge(gemm_free[t], gfree[t].at())
                                dve.bn_stats(bstat[:, t, bass.ds(cb, 1), :].rearrange("p a n -> p (a n)"), xb).then_inc(ln_stat, 1)
                                stats.step()
                        next_unit()

                if n_blocks > 1:
                    with turns(dve, n_blocks, [(split_unit, units_of_block), (step0, 4 * units_of_block), (stats, TT)]
                               + [(c, 1) for c in gfree]) as turn:
                        block(turn)
                else:
                    block(first)

            stats = Count()

            def norm_and_gate(layer):
                dve.wait_ge(ln_stat, stats.at())
                for t in range(TT):
                    ins = dve.bn_aggr(bmean[:, t, :], bstat[:, t].rearrange("p a n -> p (a n)"))
                link(ins)
                dve.tensor_scalar(rvar[:], bmean[:, :, 1], LN_EPS, None, ALU.add).then_inc(small_var, 1)
                for f in range(PLE // P):
                    aux0.step()
                    dve.wait_ge(aux_hi, hi.step())
                    freed(dve.tensor_tensor(pT[1][:, f, :], aux[f][:], pT[0][:, f, :].bitcast(F32), ALU.subtract),
                          aux_free, afree, f)
                dve.wait_ge(small_std, 2 + 2 * layer)
                link(dve.reciprocal(rvar[:], rstd[:]))
                dve.wait_ge(ln_in, 32 * (layer + 1))
                for t in range(TT):
                    link(dve.tensor_scalar(xtok[:, t, :], xtok[:, t, :], bmean[:, t, 0:1], rvar[:, t:t + 1],
                                           ALU.subtract, ALU.mult))
                    dve.tensor_tensor(xtok[:, t, :], xtok[:, t, :], ln_g[:], ALU.mult).then_inc(ln_scaled, 1)
                for t in range(TT):
                    for b in range(4):
                        split_aux_tokens(t, b)
                with turns(dve, NB // 2, [(split_unit, 10), (step0, 40)] + [(c, 2) for c in gfree + afree]) as turn:
                    for cb in range(2):
                        for u in range(5):
                            if u == 4:
                                for t in range(TT):
                                    gfree[t].step()
                                    dve.wait_ge(gemm_free[t], gfree[t].at())
                                    freed(dve.tensor_tensor(pe_g[:, t, :], aux[t][:], sig[:, t, :], ALU.mult), aux_free, afree, t)
                                    dve.wait_ge(aux_free[t], afree[t].at())
                                    xb = xtok[:, t, bass.ds(turn * 2 * BLK + cb * BLK, BLK)]
                                    dve.tensor_tensor(xb, xb, pe_g[:, t, :], ALU.add).then_inc(x_done, 1)
                            next_unit()

            dve.wait_ge(resid, 16)
            mixed(0, NB, 0, 4)
            norm_and_gate(0)

            for t in range(TT):
                for b in range(4):
                    split_aux_tokens(t, b)
            dve.memset(hp[:], 0.0).then_inc(pad_zero, 1)
            dve.wait_ge(ssd_const, 16 * 5)
            for t in range(TT):
                dve.wait_ge(gemm_steps, step0.at(t + 1))
                freed(dve.tensor_tensor(pre[0][:, t, :], gemm[t][:, 0:2 * NH], bias_row[:], ALU.add), gemm_free, gfree, t)
            next_unit()
            for t in range(TT):
                dve.wait_ge(gemm_free[t], gfree[t].at())
            dve.scalar_tensor_tensor(pre[1][:], pre[0][:], -1.0, pre[0][:], ALU.mult, ALU.max).then_inc(dt_step, 1)
            dve.wait_ge(dt_act, 2)
            link(dve.tensor_scalar(pre[2][:], pre[1][:], 2.0, None, ALU.add))
            link(dve.reciprocal(pre[3][:], pre[2][:]))
            link(dve.tensor_tensor(pre[2][:], pre[1][:], pre[3][:], ALU.mult))
            link(dve.tensor_tensor(pre[3][:], pre[2][:], pre[2][:], ALU.mult))
            acc = dt[:].rearrange("p t d h -> p t (d h)")
            link(dve.tensor_scalar(acc, pre[3][:], 1 / 15, None, ALU.mult))
            for k in (13, 11, 9, 7, 5, 3):
                link(dve.scalar_tensor_tensor(acc, acc, 1 / k, pre[3][:], ALU.add, ALU.mult))
            link(dve.scalar_tensor_tensor(acc, acc, 1.0, pre[2][:], ALU.add, ALU.mult))
            link(dve.tensor_scalar(pre[1][:], pre[0][:], 0.0, None, ALU.max))
            link(dve.scalar_tensor_tensor(acc, acc, 2.0, pre[1][:], ALU.mult, ALU.add))
            dve.scalar_tensor_tensor(aa[:], acc, -1.0, alog_row[:].unsqueeze(1).to_broadcast([P, TT, 2 * NH]),
                                     ALU.mult, ALU.mult).then_inc(dt_step, 1)
            flat = lambda v: v[:].rearrange("p t d h -> p (t d h)")
            dve.wait_ge(aux_steps, aux0.step())
            freed(dve.tensor_copy(flat(Fs), aux[0][:]), aux_free, afree, 0)
            dve.wait_ge(aux_steps, aux0.step())
            freed(dve.tensor_copy(flat(eT), aux[1][:]), aux_free, afree, 1)
            for b in range(2):
                dve.wait_ge(aux_free[b], afree[b].at())
            dve.tensor_tensor(flat(wst), flat(eT), flat(Fs), ALU.subtract).then_inc(dt_step, 1)
            dve.wait_ge(aux_steps, aux0.step())
            freed(dve.tensor_copy(FT[:], aux[2][:]), aux_free, afree, 2)
            dve.wait_ge(dt_act, 5)
            link(dve.tensor_tensor(flat(wst), flat(wst), flat(dt), ALU.mult))

            convs, xds, frs, silus, halves = Count(), Count(), [Count(), Count()], Count(), Count()

            def per_head(v):
                return v.unsqueeze(2).to_broadcast([P, HG, HD])

            def heads(v):
                return v.rearrange("p (h n) -> p h n", h=HG)

            def convolve(n, fills):
                src = hp[:, n % 4, :]
                w = lambda k: g_cw[:, n, k:k + 1]
                if n == 0 or n == 5:
                    dve.wait_ge(silu_done, silus.at(n))
                else:
                    dve.wait_ge(aux_steps, aux0.at(fill_no(fills, ("ctr", n - 1))))
                link(dve.tensor_scalar(cv[:], src[:, 0:SEQ], w(0), w(TAPS), ALU.mult, ALU.add))
                for k in range(1, TAPS):
                    ins = dve.scalar_tensor_tensor(cv[:], src[:, k:k + SEQ], w(k), cv[:], ALU.mult, ALU.add)
                    if k < TAPS - 1:
                        link(ins)
                ins.then_inc(conv_done, 1)
                convs.step()

            def half(q, fills):
                c, hf = divmod(q, 2)
                if hf == 0:
                    dve.wait_ge(aux_steps, aux0.at(fill_no(fills, ("cb", c))))
                    dve.wait_ge(weighted, halves.at())
                    dve.tensor_tensor(CBU[:], aux[0][:, 0:P], mask_le[:], ALU.mult)
                    dve.tensor_tensor(CBL[:], aux[0][:, 0:P], mask_ge[:], ALU.mult).then_inc(aux_free[0], 1)
                dve.wait_ge(fr_in[q % 2], frs[q % 2].step(32))
                for d in range(2):
                    for h in range(4):
                        e = FR[:, q % 2, d, h, :]
                        hh = 4 * hf + h
                        ins = dve.tensor_scalar(e, e, g_F[:, c, d, hh:hh + 1], 0.0, ALU.subtract, ALU.min)
                ins.then_inc(clipped, 1)
                dve.wait_ge(aux_steps, aux0.at(fill_no(fills, ("intra", q - 1)) if q else 0))
                if hf == 0:
                    dve.wait_ge(aux_free[0], free0_at(fills, c))
                for h in range(4):
                    hh = 4 * hf + h
                    ins = dve.tensor_scalar(MM[:, h, :], CBL[:], g_dt[:, c, 1, hh:hh + 1], None, ALU.mult)
                link(ins)
                for h in range(4):
                    hh = 4 * hf + h
                    ins = dve.scalar_tensor_tensor(MM[:, h, :], CBU[:], g_dt[:, c, 0, hh:hh + 1], MM[:, h, :], ALU.mult, ALU.add)
                ins.then_inc(weighted, 1)
                halves.step()

            def free0_at(fills, c):
                return base0.at(bank_no(fills, ("cb", c)))

            def state(kind, c, fills):
                bank = 2 if (kind, c) == ("back", 2) else 1
                dve.wait_ge(aux_steps, aux0.at(fill_no(fills, (kind, c))))
                for b in (1, 2):
                    dve.wait_ge(aux_free[b], base12[b].at(seen(fills, b, kind, c)))
                first = (kind, c) in (("back", 3), ("forth", 0))
                dst = st_f[:] if kind == "forth" else st_b[:, c - 1, :]
                src = st_f[:] if kind == "forth" else st_b[:, min(c, 2), :]
                if first:
                    dve.tensor_copy(dst, aux[bank][:]).then_inc(aux_free[bank], 1)
                else:
                    d = 0 if kind == "forth" else 1
                    link(dve.tensor_tensor(heads(dst), heads(src), per_head(g_tot[:, c, d, :]), ALU.mult))
                    dve.tensor_tensor(dst, dst, aux[bank][:], ALU.add).then_inc(aux_free[bank], 1)

            def seen(fills, bank, kind, c):
                at = fill_no(fills, (kind, c)) - 1
                return sum(b == bank and not second_half(n) for _, n, b in fills[:at])

            def assemble(c, fills):
                y = yg[:, c % 2, :]
                dve.wait_ge(xd_done, xds.step())
                for d, name, bank in ((0, "from_f", 1), (1, "from_b", 2)):
                    if (name, c) not in [n for _, n, _ in fills]:
                        continue
                    dve.wait_ge(aux_steps, aux0.at(fill_no(fills, (name, c))))
                    dve.tensor_tensor(heads(uu[:]), heads(aux[bank][:]), per_head(g_e[:, c, d, :]), ALU.mult).then_inc(aux_free[bank], 1)
                    dve.wait_ge(aux_free[bank], base12[bank].at(bank_no(fills, (name, c))))
                    link(dve.tensor_tensor(y, y, uu[:], ALU.add))
                dve.wait_ge(aux_steps, aux0.at(fill_no(fills, ("intra", 2 * c + 1))))
                dve.tensor_tensor(y, y, aux[3][:], ALU.add).then_inc(aux_free[3], 1)
                dve.wait_ge(aux_free[3], base3.at(c + 1))
                dve.tensor_tensor(y, y, zs[:, c, :], ALU.mult).then_inc(y_gated, 1)

            def group(g, products, ssd):
                fills = group_fills(products, ssd)
                for j in range(U_GRP):
                    if products:
                        next_unit()
                        if j == 3:
                            dve.tensor_copy(g_cw[:, 0:4, :], cw[:, bass.ds(g * 4, 4), :])
                            dve.tensor_copy(g_cw[:, 4:5, :], cw[:, bass.ds(g + DI // P, 1), :])
                            link(dve.tensor_copy(g_cw[:, 5:6, :], cw[:, bass.ds(g + DI // P + NG, 1), :]))
                    if ssd and j > 0 and j < 8:
                        half(j, fills)
                    if products:
                        if j >= 4:
                            n = j - 4
                            m = n if n < 4 else n - 2
                            dve.wait_ge(gemm_free[m], gbase[m].at(2 if n >= 4 else 1))
                            convolve(n, fills)
                    if ssd:
                        if j == 0:
                            dve.wait_ge(gemm_free[3], gbase[3].at())
                            for dst, src in ((g_F, Fs), (g_dt, dt), (g_w, wst), (g_e, eF), (g_tot, eT)):
                                dve.tensor_copy(dst[:], src[:, :, :, bass.ds((g - 1) * HG, HG)])
                            dve.tensor_copy(g_d[:], d_row[:, bass.ds((g - 1) * HG, HG)]).then_inc(group_scal, 1)
                            dve.wait_ge(group_scal, scal.step())
                            state("back", 3, fills)
                            state("back", 2, fills)
                            half(0, fills)
                        if j == 1:
                            state("back", 1, fills)
                        if j in (3, 5, 7):
                            state("forth", (j - 3) // 2, fills)
                        if j in (2, 4, 6, 8):
                            assemble((j - 2) // 2, fills)
                if products:
                    for m in range(4):
                        gbase[m].step(2 + (m >= 2))
                    silus.step(GCH)
                aux0.step(len(fills))
                base0.step(bank_count(fills, 0))
                base12[1].step(bank_count(fills, 1))
                base12[2].step(bank_count(fills, 2))
                base3.step(bank_count(fills, 3))

            scal = Count()
            gbase = gfree
            base0, base3, base12 = Count(afree[0].n), Count(afree[3].n), {b: Count(afree[b].n) for b in (1, 2)}
            both = group_fills(True, True)
            group(0, True, False)
            with turns(dve, NG // 2 - 1, [(split_unit, 2 * U_GRP), (step0, 8 * U_GRP), (aux0, 2 * len(both)),
                       (base0, 2 * bank_count(both, 0)), (base3, 2 * bank_count(both, 3)),
                       (base12[1], 2 * bank_count(both, 1)), (base12[2], 2 * bank_count(both, 2)), (convs, 2 * GCH),
                       (silus, 2 * GCH), (xds, 8), (scal, 2), (halves, 16), (frs[0], 256), (frs[1], 256), (order, ORDER_2)]
                       + [(gbase[m], 4 + 2 * (m >= 2)) for m in range(4)]) as turn:
                group(turn * 2 + 1, True, True)
                group(turn * 2 + 2, True, True)
            group(NG - 1, True, True)
            group(NG, False, True)
            for b, c in ((0, base0), (1, base12[1]), (2, base12[2]), (3, base3)):
                afree[b].n = c.n

            dve.wait_ge(y_squared, NG * TT)
            link(dve.tensor_reduce(stat[:, 96:100], ssq, AX.X, ALU.add))
            dve.tensor_scalar(stat[:, 100:104], stat[:, 96:100], 1.0 / DI, RMS_EPS, ALU.mult, ALU.add).then_inc(small_var, 1)
            dve.wait_ge(small_std, 3)
            link(dve.reciprocal(stat[:, 108:112], stat[:, 104:108]))
            n = 0
            for q in (7, 0, 1, 2, 3, 4, 5, 6):
                for k in range(4 * q, 4 * q + 4):
                    n += 1
                    dve.wait_ge(y_hi, n)
                    dve.scalar_tensor_tensor(y_part(1, k), y_raw(k), smalls[:, 8 + k:9 + k], y_part(0, k).bitcast(F32),
                                             ALU.mult, ALU.subtract).then_inc(y_lo, 1)
            dve.wait_ge(alpha_done, 1)
            mixed(1, NB - 1, 0, 8)
            dve.wait_ge(alpha_done, 2)
            mixed(1, 1, NB - 1, 8)
            norm_and_gate(1)

        @block.gpsimd
        def _(pool):
            order = Count()

            def link(ins):
                ins.then_inc(pool_order, 1)
                pool.wait_ge(pool_order, order.step())

            def rotate(dst, src, c, s, a, b, done):
                pool.tensor_tensor(a, src[0], c, ALU.mult)
                link(pool.tensor_tensor(b, src[1], s, ALU.mult))
                link(pool.tensor_tensor(dst[0], a, b, ALU.subtract))
                pool.tensor_tensor(a, src[1], c, ALU.mult)
                link(pool.tensor_tensor(b, src[0], s, ALU.mult))
                pool.tensor_tensor(dst[1], a, b, ALU.add).then_inc(done, 1)

            pool.wait_ge(trig_done, 2)
            for t in range(TT):
                pool.wait_ge(gemm_free[t], 3)
            for copy in range(2):
                if copy:
                    pool.wait_ge(k_rotated, copy)
                h = ROPE // 2
                rotate([k_rot[:, :, copy, 0:h], k_rot[:, :, copy, h:]], [k_tok[:, :, 0:h], k_tok[:, :, h:]],
                       cos[:], sin[:], rk_a[:], rk_b[:], k_rotated)
            pairs = Count()
            cb = cos[:].unsqueeze(2).to_broadcast([P, TT, 2, ROPE // 2])
            sb_ = sin[:].unsqueeze(2).to_broadcast([P, TT, 2, ROPE // 2])
            turned = Count(TT + 2 - 4)
            g2 = Count(7)
            with turns(pool, PAIRS, [(order, 3), (pairs, 1), (turned, 5), (g2, 2)]):
                pool.wait_ge(gemm_free[2], g2.at(1))
                pool.wait_ge(q_rotated, pairs.at())
                pool.wait_ge(aux_free[3], turned.at())
                rotate([q_rot[:, :, :, 0, :], q_rot[:, :, :, 1, :]], [q_tok[:, :, :, 0, :], q_tok[:, :, :, 1, :]],
                       cb, sb_, rope_a[:], rope_b[:], q_rotated)
                pairs.step(), turned.step(5), g2.step(2)

            def shift(layer):
                pool.wait_ge(ln_in, 32 * (layer + 1))
                for t in range(TT):
                    pool.wait_ge(ln_scaled, layer * TT + t + 1)
                    pool.tensor_tensor(xtok[:, t, :], xtok[:, t, :], ln_b[:], ALU.add).then_inc(ln_done, 1)

            shift(0)

            def per_head(v):
                return v.unsqueeze(2).to_broadcast([P, HG, HD])

            def heads(v):
                return v.rearrange("p (h n) -> p h n", h=HG)

            scal, silus, clips, muls, squares, ends = Count(), Count(), Count(), Count(), Count(), Count()
            aux0 = Count(AUX_SSD)
            xdn, xwn = Count(), Count()

            def weigh(o, c, d, buf):
                pool.tensor_tensor(heads(Xw[:, buf, :]), heads(X[:, o, c, :]), per_head(g_w[:, c, d, :]), ALU.mult).then_inc(xw_done, 1)

            def group(s, products):
                o = 1 - s
                fills = group_fills(products, True)
                pool.wait_ge(group_scal, scal.step())
                pool.wait_ge(silu_done, silus.step(GCH))
                for j in range(8):
                    if j == 0:
                        weigh(o, 3, 1, 0)
                        weigh(o, 2, 1, 1)
                    if j == 1:
                        pool.wait_ge(aux_steps, aux0.at(fill_no(fills, ("back", 3))))
                        weigh(o, 1, 1, 0)
                    if j in (2, 4, 6):
                        c = (j - 2) // 2
                        before = [("back", 1), ("back", 2), ("forth", 0)][c]
                        pool.wait_ge(aux_steps, aux0.at(fill_no(fills, before)))
                        weigh(o, c, 0, c % 2)
                    pool.wait_ge(clipped, clips.step())
                    pool.wait_ge(mixed_m, muls.at())
                    pool.tensor_tensor(EX[:], FR[:, j % 2, 0], FR[:, j % 2, 1], ALU.add).then_inc(summed, 1)
                    pool.wait_ge(decayed, clips.at())
                    pool.wait_ge(weighted, clips.at())
                    pool.tensor_tensor(MM[:], MM[:], EX[:], ALU.mult).then_inc(mixed_m, 1)
                    muls.step()
                    if j in (0, 3, 5, 7):
                        c = j // 2
                        pool.wait_ge(y_squared, squares.at())
                        pool.tensor_tensor(heads(yg[:, c % 2, :]), heads(X[:, o, c, :]), per_head(g_d[:]), ALU.mult).then_inc(xd_done, 1)
                        squares.step()
                aux0.step(len(fills))

            both = group_fills(True, True)
            aux0.step(sum(n[0] == "ctr" for _, n, _ in both))
            with turns(pool, NG // 2 - 1, [(scal, 2), (silus, 2 * GCH), (clips, 16), (muls, 16), (squares, 8), (aux0, 2 * len(both))]):
                group(1, True)
                group(0, True)
            group(1, True)
            group(0, False)
            for n in range(2):
                pool.wait_ge(resid1, 16 * (n + 1))
                cols = slice(0, D - BLK) if n == 0 else slice(D - BLK, D)
                pool.tensor_scalar(xtok[:, :, cols], xtok[:, :, cols], ALPHA, 1.0, ALU.mult, ALU.mult).then_inc(alpha_done, 1)
            shift(1)


def layout(inputs):
    f = lambda n: np.asarray(inputs[n])
    units = []

    def add(w, k_tiles, cols):
        per = max(1, UNIT // cols)
        w = w.reshape(k_tiles, P, cols)
        for k in range(0, k_tiles, per):
            u = w[k:k + per].transpose(1, 0, 2).reshape(P, -1)
            if u.shape[1] < UNIT:
                u = np.concatenate([u, np.zeros((P, UNIT - u.shape[1]), u.dtype)], 1)
            units.append(u)

    def blocks(w, n=BLK):
        for c in range(0, w.shape[1], n):
            add(w[:, c:c + n], w.shape[0] // P, n)

    def gate(layer):
        for c in range(0, D, BLK):
            add(f("ple_w_proj")[layer][:, c:c + BLK], PLE // P, BLK)
            add(f("ple_w_gate")[layer][:, c:c + BLK], KD, BLK)

    w = f("mla_w_in")[0]
    blocks(w[:, 0:2 * LORA])
    add(w[:, 2 * LORA:2 * LORA + ROPE], KD, ROPE)
    blocks(w[:, 2 * LORA + ROPE:])
    for g in range(PAIRS):
        u = f("mla_w_uq")[0][:, g * 2 * QKH:(g + 1) * 2 * QKH].reshape(KL, P, 2 * QKH).transpose(1, 0, 2).reshape(P, -1)
        units.append(np.concatenate([u, np.zeros((P, UNIT - u.shape[1]), u.dtype)], 1))
        add(f("mla_w_ukv")[0][:, g * 2 * (NOPE + VH):(g + 1) * 2 * (NOPE + VH)], KL, 2 * (NOPE + VH))
    blocks(f("mla_w_o")[0])
    gate(0)
    w = f("ssd_w_in")[0]
    z0, x0, b0, c0, d0 = 0, DI, 2 * DI, 2 * DI + NG * NS, 2 * DI + 2 * NG * NS
    add(w[:, d0:], KD, 2 * NH)
    for g in range(NG):
        blocks(w[:, x0 + g * BLK:x0 + (g + 1) * BLK])
        add(np.concatenate([w[:, b0 + g * NS:b0 + (g + 1) * NS], w[:, c0 + g * NS:c0 + (g + 1) * NS]], 1), KD, 2 * NS)
        blocks(w[:, z0 + g * BLK:z0 + (g + 1) * BLK])
    w = f("ssd_w_out")[0]
    rows = np.r_[DI - BLK:DI, 0:DI - BLK]
    blocks(w[rows])
    gate(1)
    units += [np.zeros((P, UNIT), np.float32)] * 2
    return np.stack(units)


def kernel(**inputs):
    import concourse.bacc as bacc
    from concourse.bass_utils import run_bass_kernel_spmd

    arrays = layout_all(inputs)
    nc = bacc.Bacc("TRN2", target_bir_lowering=False, num_devices=1)
    args = [nc.dram_tensor(n, a.shape, mybir.dt.from_np(a.dtype), kind="ExternalInput").ap() for n, a in arrays.items()]
    out = nc.dram_tensor("out_dram", (SEQ, D), F32, kind="ExternalOutput").ap()
    trunk(nc, *args, out)
    r = run_bass_kernel_spmd(nc, [arrays], core_ids=[0])
    return r.results[0]["out_dram"].reshape(1, SEQ, D)


def layout_all(inputs):
    f = lambda n: np.asarray(inputs[n])
    a = np.arange(P)
    consts = np.stack([np.eye(P), a[:, None] <= a[None, :], a[:, None] >= a[None, :], np.ones((P, P))]).astype(np.float32)
    invf = 1.0 / (np.float32(10000.0) ** (np.arange(0, ROPE, 2, dtype=np.float32) / np.float32(ROPE)))
    chunks = lambda v: v.reshape(-1, P).T
    small = np.concatenate([chunks(f("mla_q_norm")[0]), chunks(f("mla_kv_norm")[0]), chunks(f("ssd_norm")[0])], 1)
    lnw = np.stack([f("ln_g")[0], f("ln_b")[0], f("ln_g")[1], f("ln_b")[1]])
    convw = np.concatenate([f("ssd_conv_w")[0], f("ssd_conv_b")[0][None]], 0)
    convw = convw.reshape(TAPS + 1, -1, P).transpose(2, 1, 0)
    rows = np.concatenate([invf, f("ssd_dt_bias")[0].ravel(), f("ssd_a_log")[0].ravel(), f("ssd_d")[0]])[None]
    return {
        "x_dram": f("x")[0], "p_dram": f("p")[:, 0], "pos_dram": np.ascontiguousarray(f("positions").reshape(TT, P).T),
        "consts_dram": consts, "ln_dram": lnw, "weights_dram": layout(inputs), "small_dram": np.ascontiguousarray(small),
        "conv_dram": np.ascontiguousarray(convw), "rows_dram": rows.astype(np.float32),
    }
```

```python
from contextlib import ExitStack, contextmanager

import numpy as np
import concourse.bass as bass
from concourse import mybir

F32 = mybir.dt.float32
F32R = mybir.dt.float32r
I32 = mybir.dt.int32
ACT = mybir.ActivationFunctionType
ALU = mybir.AluOpType
AX = mybir.AxisListType

P = 128
D = 2048
SEQ = 512
TT = SEQ // P
KD = D // P
BLK = 512
NB = D // BLK
UNIT = 2048
KU = UNIT // BLK
PLE = 256
HEADS, NOPE, ROPE, VH = 16, 128, 64, 128
QKH = NOPE + ROPE
LORA = 512
KL = LORA // P
SCALE = QKH ** -0.5
ALPHA = 4 ** 0.25
LN_EPS, RMS_EPS = 1e-5, 1e-6
DI = 4096
NH, HD, NG, HG, NS = 64, 64, 8, 8, 128
TAPS = 7
PAD = TAPS // 2
PAIRS = HEADS // 2
GCH = 6
U_CQ, U_CKV, U_KR, U_Z, U_ATT, U_O, U_GATE = 4, 4, 1, 16, 2 * PAIRS, 16, 20
U_DT, U_GRP, U_OUT = 1, 10, 32
Y_SLOTS = (2, 4, 6, 9)
Y_STEPS = {1: 0, 2: 1, 4: 2, 6: 3}
Y_FIRST = [0, 4, 8, 12, 28, 16, 20, 24]
Y_ORDER = [28, 16, 20, 24, 0, 4, 8, 12]
UNITS = U_CQ + U_CKV + U_KR + U_Z + U_ATT + U_O + U_GATE + U_DT + NG * U_GRP + U_OUT + U_GATE

TWO_PI_PARTS = (6.28125, 0.0019350051879882812, 3.0199159819567e-07)
ROUND = 12582912.0
PI32 = 3.1415925
AHEAD = {0: 1, 1: 2, 2: 3, 3: 4, 5: 5, 6: 6}
AUX2_ATT = TT + 2 + 6 * PAIRS
ORDER_2 = 2 * (1 + GCH * (TAPS - 1) + 8 + TT + 2 + 2 + 6)
AUX_SSD = 3 * 4 * TT + 1 + 2 * KL + 1 + PAIRS * 19 + 2 + 4
AUX0_SSD = 3 * TT + 4 + PAIRS + 1 + NB + 1


def group_fills(products, ssd):
    f = []
    for j in range(U_GRP):
        if products and j >= 5:
            f.append((j, ("ctr", j - 5), 2 if j % 2 else 0))
        if ssd:
            if 1 <= j <= 8:
                f.append((j, ("intra", j - 1), 3))
            if j == 0:
                f += [(j, ("cb", 0), 0), (j, ("back", 3), 1), (j, ("back", 2), 2)]
            if j == 1:
                f.append((j, ("back", 1), 1))
            if j in (3, 5, 7):
                f.append((j, ("forth", (j - 3) // 2), 1))
            if j in (2, 4, 6, 8):
                c = (j - 2) // 2
                f += [(j, ("from_f", c), 1)] * (c > 0) + [(j, ("from_b", c), 2)] * (c < TT - 1)
            if j in (3, 5, 7, 9):
                f.append((j, ("ytr", (j - 3) // 2), 0))
    return f


def bank_no(fills, name):
    bank = next(b for _, n, b in fills if n == name)
    mine = [n for _, n, b in fills if b == bank and not second_half(n)]
    return mine.index(name) + 1


def bank_count(fills, bank):
    return sum(b == bank and not second_half(n) for _, n, b in fills)


def second_half(name):
    return name[0] == "intra" and name[1] % 2 == 1


def fill_no(fills, name):
    return [n for _, n, _ in fills].index(name) + 1


def slot_uses(c):
    first = 16 * (c.n // 2 + 1)
    return first if c.turn is None else c.turn * (8 * c.per) + first


class Count:

    def __init__(self, n=0):
        self.n, self.turn, self.per = n, None, 0

    def at(self, ahead=0):
        v = self.n + ahead
        return v if self.turn is None else self.turn * self.per + v

    def step(self, k=1):
        self.n += k
        return self.at()


@contextmanager
def turns(eng, n, per_turn):
    with eng.Fori(0, n) as turn:
        start = [c.n for c, _ in per_turn]
        for c, per in per_turn:
            c.turn, c.per = turn, per
        yield turn
    for (c, per), first in zip(per_turn, start):
        assert c.n == first + per, (c.n - first, per)
        c.turn, c.n = None, first + n * per


def trunk(nc, x, p, positions, consts, lnw, wstream, small, convw, rows, out):
    base = nc.sbuf_base + (-nc.sbuf_base) % 64

    with ExitStack() as ctx:
        def at(name, kb, shape, dt=F32):
            return nc.alloc_sbuf_tensor_at(name, shape, dt, offset=base + int(kb * 1024))

        def sem(name):
            return ctx.enter_context(nc.semaphore(name))

        xT = [at("xT_hi", 0, [P, KD, SEQ], F32R), at("xT_lo", 32, [P, KD, SEQ], F32R)]
        xtok = at("xtok", 64, [P, TT, D])
        raw = at("raw", 96, [P, 2, UNIT])
        W = [at("w_hi", 112, [P, 2, UNIT], F32R), at("w_lo", 128, [P, 2, UNIT], F32R)]
        ident = at("ident", 144, [P, P])
        mask_le = at("mask_le", 144.5, [P, P])
        mask_ge = at("mask_ge", 145, [P, P])
        smalls = at("smalls", 145.5, [P, 8 + 32])
        stat = at("stat", 146, [P, 256])
        PT = at("PT", 0, [P, 2, TT, SEQ])
        prob = at("prob", 16, [P, 2, SEQ])
        q_tok = at("q_tok", 20, [P, TT, 2, 2, ROPE // 2])
        q_rot = at("q_rot", 22, [P, TT, 2, 2, ROPE // 2])
        rope_a = at("rope_a", 24, [P, TT, 2, ROPE // 2])
        rope_b = at("rope_b", 25, [P, TT, 2, ROPE // 2])
        qrT = at("qrT", 26, [P, 2, SEQ])
        krT = at("krT", 30, [P, SEQ])
        g_raw = at("g_raw", 32, [P, KD, SEQ])
        zT = at("zT", 64, [P, KD, SEQ])
        cT = [at("cT_hi", 148, [P, 2 * KL, SEQ], F32R), at("cT_lo", 164, [P, 2 * KL, SEQ], F32R)]
        qT = at("qT", 180, [P, 2, 2, SEQ])
        kT = at("kT", 188, [P, 2, 2, SEQ])
        v_tok = at("v_tok", 196, [P, 2, TT, 2 * VH])
        cos = at("cos", 204, [P, TT, ROPE // 2])
        sin = at("sin", 204.5, [P, TT, ROPE // 2])
        c_tok = at("c_tok", 180, [P, 2, TT, LORA])
        k_tok = at("k_tok", 196, [P, TT, ROPE])
        k_rot = at("k_rot", 197, [P, TT, 2, ROPE])
        rk_a = at("rk_a", 205, [P, TT, ROPE // 2])
        rk_b = at("rk_b", 205.5, [P, TT, ROPE // 2])
        junk = at("junk", 199, [P, SEQ])
        kF = at("kF", 199, [P, SEQ])
        trig = at("trig", 201, [P, 4, TT * ROPE // 2])
        invf = at("invf", 203, [P, ROPE // 2])
        pos_i = at("pos_i", 203.25, [P, TT], I32)
        pos_f = at("pos_f", 203.5, [P, TT])
        ln_g = at("ln_g", 148, [P, D])
        ln_b = at("ln_b", 156, [P, D])
        p_tok = at("p_tok", 164, [P, TT, PLE])
        pT = [at("pT_hi", 168, [P, PLE // P, SEQ], F32R), at("pT_lo", 172, [P, PLE // P, SEQ], F32R)]
        sig = at("sig", 176, [P, TT, BLK])
        pe_g = at("pe_g", 184, [P, TT, BLK])
        bstat = at("bstat", 205, [P, TT, NB, 6])
        bmean = at("bmean", 205.5, [P, TT, 2])
        rstd = at("rstd", 205.75, [P, TT])
        rvar = at("rvar", 205.875, [P, TT])
        shift = at("shift", 205.9375, [P, TT])
        FR = at("FR", 64, [P, 2, 2, 4, P])
        wst = at("wst", 72, [P, TT, 2, NH])
        CB = at("CB", 74, [P, TT, P])
        MM = [at("MM0", 76, [P, 4, P]), at("MM1", 174, [P, 4, P])]
        CBU = at("CBU", 78, [P, P])
        CBL = at("CBL", 78.5, [P, P])
        st_b = at("st_b", 79, [P, 3, BLK])
        st_f = at("st_f", 85, [P, BLK])
        Xw = at("Xw", 87, [P, 2, BLK])
        uu = at("uu", 91, [P, BLK])
        Fs = at("Fs", 93, [P, TT, 2, NH])
        g_tot = at("g_tot", 95, [P, TT, 2, HG])
        g_d = at("g_d", 95.25, [P, HG])
        d_row = at("d_row", 145.71875, [P, NH])
        g_F = at("g_F", 147, [P, TT, 2, HG])
        g_dt = at("g_dt", 147.25, [P, TT, 2, HG])
        g_w = at("g_w", 147.5, [P, TT, 2, HG])
        g_e = at("g_e", 147.75, [P, TT, 2, HG])
        X = at("X", 148, [P, 2, TT, BLK])
        zs = at("zs", 164, [P, TT, BLK])
        BT = at("BT", 172, [P, SEQ])
        CT = at("CT", 176, [P, 2, SEQ])
        Bt = at("Bt", 180, [P, 2, TT, NS])
        hp = at("hp", 184, [P, 4, SEQ + 2 * PAD])
        cv = at("cv", 192.25, [P, SEQ])
        eT = at("eT", 194.25, [P, TT, 2, NH])
        cw = at("cw", 196.25, [P, DI // P + 2 * NG, TAPS + 1])
        yg = at("yg", 197.75, [P, 2, BLK])
        yTc = at("yTc", 201.75, [P, 4, P])
        dt = at("dt", 203.75, [P, TT, 2, NH])
        eF = at("eF", 205.75, [P, TT, 2, NH])
        pre = [at(f"pre{i}", kb, [P, TT, 2 * NH]) for i, kb in enumerate((64, 66, 68, 70))]
        ones = at("ones", 76, [P, P])
        bias_row = at("bias_row", 78, [P, 2 * NH])
        alog_row = at("alog_row", 78.5, [P, 2 * NH])
        aa = at("aa", 80, [P, TT, 2 * NH])
        FT = at("FT", 82, [P, SEQ])
        yA = [at("yA_hi", 0, [P, KD, SEQ], F32R), at("yA_lo", 32, [P, KD, SEQ], F32R)]
        yB = [at("yB_hi", 148, [P, 12, SEQ], F32R), at("yB_lo", 172, [P, 12, SEQ], F32R)]
        yC = [at("yC_hi", 196, [P, 4, SEQ], F32R), at("yC_lo", 64, [P, TT, D], F32R)]
        yA_raw = at("yA_raw", 32, [P, KD, SEQ])
        yB_raw = at("yB_raw", 172, [P, 12, SEQ])
        yC_raw = at("yC_raw", 64, [P, TT, D])

        def y_part(i, k):
            if k < 16:
                return yA[i][:, k, :]
            if k < 28:
                return yB[i][:, k - 16, :]
            return yC[0][:, k - 28, :] if i == 0 else yC[1][:, k - 28, D - BLK:]

        def y_raw(k):
            return yA_raw[:, k, :] if k < 16 else yB_raw[:, k - 16, :] if k < 28 else yC_raw[:, k - 28, D - BLK:]

        def y_raw_quad(q):
            if q < 4:
                return yA_raw[:, 4 * q:4 * q + 4, :]
            return yB_raw[:, 4 * q - 16:4 * q - 12, :] if q < 7 else yC_raw[:, :, D - BLK:]

        g_cw = at("g_cw", 95.5, [P, GCH, TAPS + 1])
        ssq = stat[:, 64:64 + TT * NG].rearrange("p (c g) -> p c g", c=TT)
        x_mid = nc.dram_tensor("x_mid", (SEQ, D), F32, kind="Internal").ap()
        f_rows = nc.dram_tensor("f_rows", (2 * NH, SEQ), F32, kind="Internal").ap()
        y_scr = nc.dram_tensor("y_scr", (NG, P, 4, SEQ), F32, kind="Internal").ap()

        gemm = [ctx.enter_context(nc.psum_tensor(f"gemm{m}", [P, BLK], F32)) for m in range(4)]
        aux = [ctx.enter_context(nc.psum_tensor(f"aux{m}", [P, BLK], F32)) for m in range(4)]

        const_in = sem("const_in")
        x_in = [sem(f"x_in{t}") for t in range(TT)]
        raw_in = [sem(f"raw_in{s}") for s in range(2)]
        hi_done = sem("hi_done")
        split_done = sem("split_done")
        gemm_steps = sem("gemm_steps")
        aux_steps = sem("aux_steps")
        gemm_free = [sem(f"gemm_free{m}") for m in range(4)]
        aux_free = [sem(f"aux_free{m}") for m in range(4)]
        aux_hi = sem("aux_hi")
        dve_order = sem("dve_order")
        pool_order = sem("pool_order")
        ssq_done = sem("ssq_done")
        small_var = sem("small_var")
        small_std = sem("small_std")
        c_normed = sem("c_normed")
        trig_arg, trig_done = sem("trig_arg"), sem("trig_done")
        k_rotated = sem("k_rotated")
        q_rotated = sem("q_rotated")
        max_done, exp_done, norm_done = sem("max_done"), sem("exp_done"), sem("norm_done")
        g_split = sem("g_split")
        ln_in = sem("ln_in")
        resid = sem("resid")
        ln_stat, ln_scaled, ln_done = sem("ln_stat"), sem("ln_scaled"), sem("ln_done")
        ln_rstd = sem("ln_rstd")
        ln_centred = sem("ln_centred")
        x_done = sem("x_done")
        out_done = sem("out_done")
        p_in = sem("p_in")
        spill, ssd_const, alpha_done, resid1 = sem("spill"), sem("ssd_const"), sem("alpha_done"), sem("resid1")
        pad_zero = sem("pad_zero")
        dt_step = sem("dt_step")
        dt_act = sem("dt_act")
        ft_out = sem("ft_out")
        conv_done, silu_done = sem("conv_done"), sem("silu_done")
        fr_in = [sem("fr_in0"), sem("fr_in1")]
        group_scal = sem("group_scal")
        clipped = sem("clipped")
        summed = sem("summed")
        decayed = sem("decayed")
        weighted = sem("weighted")
        mixed_m = sem("mixed_m")
        xw_done = sem("xw_done")
        xd_done = sem("xd_done")
        y_gated = sem("y_gated")
        y_squared = sem("y_squared")
        y_out = sem("y_out")
        y_in = [sem(f"y_in{q}") for q in range(8)]
        y_hi, y_lo = sem("y_hi"), sem("y_lo")

        block = ctx.enter_context(nc.Block())

        def layer_norm_loads(sp, layer):
            if layer:
                sp.wait_ge(gemm_steps, 4 * (UNITS - U_GATE - 4))
            sp.dma_start(ln_g[:], lnw[2 * layer:2 * layer + 1, :].to_broadcast([P, D])).then_inc(ln_in, 16)
            sp.dma_start(ln_b[:], lnw[2 * layer + 1:2 * layer + 2, :].to_broadcast([P, D])).then_inc(ln_in, 16)
            sp.dma_start(p_tok[:], p[layer].rearrange("(t p) n -> p t n", p=P)).then_inc(p_in, 16)

        @block.sync
        def _(sp):
            unit = Count()

            def load_units(n):
                pairs, one = divmod(n - (unit.n % 2), 2)
                if unit.n % 2:
                    load_unit(unit.n)
                if pairs:
                    first = unit.n
                    if first == 0:
                        load_unit(0)
                        load_unit(1)
                        pairs -= 1
                    if pairs:
                        with turns(sp, pairs, [(unit, 2)]) as turn:
                            for s in range(2):
                                sp.wait_ge(split_done, unit.at(-1))
                                sp.dma_start(raw[:, s, :], wstream[bass.ds(unit.at(), 1), :, :]
                                             .rearrange("a p n -> p (a n)")).then_inc(raw_in[s], 16)
                                unit.step()
                if one:
                    load_unit(unit.n)

            def load_unit(u):
                if u >= 2:
                    sp.wait_ge(split_done, u - 1)
                sp.dma_start(raw[:, u % 2, :], wstream[u]).then_inc(raw_in[u % 2], 16)
                unit.step()

            for dst, n in ((ident, 0), (mask_le, 1), (mask_ge, 2)):
                sp.dma_start(dst[:], consts[n]).then_inc(const_in, 16)
            sp.dma_start(smalls[:], small).then_inc(const_in, 16)
            sp.dma_start(invf[:], rows[0:1, 0:ROPE // 2].to_broadcast([P, ROPE // 2])).then_inc(const_in, 16)
            sp.dma_start(pos_i[:], positions).then_inc(const_in, 16)
            for t in range(TT):
                sp.dma_start(xtok[:, t, :], x[t * P:(t + 1) * P, :]).then_inc(x_in[t], 16)
            load_units(U_CQ + U_CKV + U_KR + U_Z + U_ATT)
            load_units(4)
            sp.wait_ge(g_split, 4)
            sp.dma_start(xtok[:], x.rearrange("(t p) n -> p t n", p=P)).then_inc(resid, 16)
            layer_norm_loads(sp, 0)
            load_units(U_O - 4 + U_GATE + U_DT)
            load_units(2)
            load_units(NG * U_GRP - 2 + U_OUT + 2)
            layer_norm_loads(sp, 1)
            load_units(U_GATE)
            for n, cols in enumerate((slice(0, D - BLK), slice(D - BLK, D))):
                sp.wait_ge(x_done, (2 * NB - 1 + n) * TT)
                sp.dma_start(out.rearrange("(t p) n -> p t n", p=P)[:, :, cols], xtok[:, :, cols]).then_inc(out_done, 16)
            sp.wait_ge(out_done, 32)

        @block.tensor
        def _(pe):
            gfree = [Count() for _ in range(4)]
            afree = [Count() for _ in range(4)]
            units = Count()

            def passes(o, w, a, start, stop, swap=False):
                for n, (i, j) in enumerate(((0, 0), (0, 1), (1, 0))):
                    l, r = (a[j], w[i]) if swap else (w[i], a[j])
                    mm = pe.matmul(o, l, r, start=start and n == 0, stop=stop and n == 2)
                return mm

            def begin_unit():
                pe.wait_ge(split_done, units.step())

            def take_gemm(m):
                pe.wait_ge(gemm_free[m], gfree[m].at())
                gfree[m].step()

            def take_aux(m):
                pe.wait_ge(aux_free[m], afree[m].at())
                afree[m].step()

            def aux_read():
                for m in range(4):
                    pe.wait_ge(aux_free[m], afree[m].at())

            def product(*args, **kw):
                for _ in product_units(*args, **kw):
                    pass

            def product_units(acts, k_tiles, tokens_out, banks=None, take=take_gemm, order=None, ready=None):
                ku = UNIT // BLK
                first = order[0] if order else 0
                last = (order[-1] if order else (k_tiles - 1) // ku * ku) + min(ku, k_tiles) - 1
                if isinstance(acts, list):
                    acts = (lambda parts: lambda i, k: parts[i][:, k, :])(acts)
                for n, k0 in enumerate(order or range(0, k_tiles, ku)):
                    slot = units.n % 2
                    begin_unit()
                    if ready:
                        pe.wait_ge(*ready(n))
                    kn = min(ku, k_tiles - k0)
                    for m in range(4):
                        if k0 == first:
                            take(m)
                        for k in range(kn):
                            sl = slice(k * BLK, (k + 1) * BLK) if tokens_out else slice(k * BLK + m * P, k * BLK + (m + 1) * P)
                            w = [W[i][:, slot, sl] for i in range(2)]
                            a = [acts(i, k0 + k)[:, m * P:(m + 1) * P] if tokens_out else acts(i, k0 + k) for i in range(2)]
                            mm = passes((banks or gemm)[m][:], w, a, k0 + k == first, k0 + k == last, swap=tokens_out)
                        mm.then_inc(gemm_steps, 1)
                    yield

            def transpose_tokens():
                for t in range(TT):
                    yield t
                    for b in range(4):
                        take_aux(b)
                        for k in range(4):
                            f = 4 * b + k
                            tr = pe.transpose(aux[b][:, k * P:(k + 1) * P], xtok[:, t, f * P:(f + 1) * P], ident[:])
                        tr.then_inc(aux_steps, 1)

            pe.wait_ge(const_in, 16 * 6)
            for t in transpose_tokens():
                pe.wait_ge(x_in[t], 16)
            aux_read()
            product(xT, KD, True)
            product(xT, KD, True)
            slot = units.n % 2
            begin_unit()
            take_gemm(0)
            for k in range(KD):
                mm = passes(gemm[0][0:ROPE, :], [w[:, slot, k * ROPE:(k + 1) * ROPE] for w in W],
                            [x[:, k, :] for x in xT], k == 0, k == KD - 1)
                if k % 4 == 3:
                    mm.then_inc(gemm_steps, 1)
            pe.wait_ge(gemm_free[0], gfree[0].at())
            take_aux(0)
            for t in range(TT):
                tr = pe.transpose(aux[0][:, t * ROPE:(t + 1) * ROPE], kF[0:ROPE, t * P:(t + 1) * P], ident[0:ROPE, 0:ROPE])
            tr.then_inc(aux_steps, 1)
            with turns(pe, NB, [(c, 1) for c in gfree] + [(units, 4)]):
                product(xT, KD, False)
            pe.wait_ge(c_normed, 2 * TT)
            for f in range(2 * KL):
                take_aux(f % 4)
                for t in range(TT):
                    tr = pe.transpose(aux[f % 4][:, t * P:(t + 1) * P],
                                      c_tok[:, f // KL, t, (f % KL) * P:(f % KL + 1) * P], ident[:])
                tr.then_inc(aux_steps, 1)
            pe.wait_ge(k_rotated, 2)
            take_aux(0)
            for t in range(TT):
                tr = pe.transpose(aux[0][:, t * P:(t + 1) * P], k_rot[:, t].rearrange("p a b -> p (a b)"), ident[:])
            tr.then_inc(aux_steps, 1)
            aux_read()

            norm_seen, q_seen = Count(), Count(1)

            def qkv():
                slot = units.n % 2
                begin_unit()
                wq = [W[i][:, slot, 0:KL * 2 * QKH].rearrange("p (k h n) -> p k h n", k=KL, h=2) for i in range(2)]
                for h in range(2):
                    take_gemm(h)
                    for k in range(KL):
                        mm = passes(gemm[h][:], [w[:, k, h, 0:NOPE] for w in wq], [c[:, k, :] for c in cT],
                                    k == 0, k == KL - 1)
                    mm.then_inc(gemm_steps, 1)
                    yield
                take_gemm(2)
                for t in range(TT):
                    for k in range(KL):
                        mm = passes(gemm[2][:, t * 2 * ROPE:(t + 1) * 2 * ROPE], [w[:, k, :, NOPE:QKH] for w in wq],
                                    [c[:, k, t * P:(t + 1) * P] for c in cT], k == 0, k == KL - 1, swap=True)
                    if t % 2:
                        mm.then_inc(gemm_steps, 1)
                yield
                slot = units.n % 2
                begin_unit()
                wk = [W[i][:, slot, :].rearrange("p (k h n) -> p k h n", k=KL, h=2) for i in range(2)]
                for h, m in ((0, 3), (1, 0)):
                    take_gemm(m)
                    for k in range(KL):
                        mm = passes(gemm[m][:], [w[:, k, h, 0:NOPE] for w in wk], [c[:, KL + k, :] for c in cT],
                                    k == 0, k == KL - 1)
                    mm.then_inc(gemm_steps, 1)
                    yield
                for m in (1, 2):
                    take_gemm(m)
                    for j in range(2):
                        t = 2 * (m - 1) + j
                        for k in range(KL):
                            mm = passes(gemm[m][:, j * 2 * VH:(j + 1) * 2 * VH], [w[:, k, :, NOPE:] for w in wk],
                                        [c[:, KL + k, t * P:(t + 1) * P] for c in cT], k == 0, k == KL - 1, swap=True)
                    mm.then_inc(gemm_steps, 1)
                    yield

            def turn_queries():
                pe.wait_ge(q_rotated, q_seen.step())
                take_aux(0)
                for t in range(TT):
                    tr = pe.transpose(aux[0][:, t * P:(t + 1) * P], q_rot[:, t].rearrange("p h a b -> p (h a b)"), ident[:])
                tr.then_inc(aux_steps, 1)

            def attend(s, ahead):
                steps = iter(qkv() if ahead else ())
                pe.wait_ge(aux_free[0], afree[0].at())

                def scores(n):
                    h, t = divmod(n, TT)
                    pe.matmul(aux[n % 2][:], qT[:, s, h, t * P:(t + 1) * P], kT[:, s, h, :], start=True, stop=False)
                    pe.matmul(aux[n % 2][:], qrT[h * ROPE:(h + 1) * ROPE, s, t * P:(t + 1) * P],
                              krT[h * ROPE:(h + 1) * ROPE, :], start=False, stop=True).then_inc(aux_steps, 1)

                def turn_probs(n):
                    pe.wait_ge(norm_done, norm_seen.step())
                    take_aux(2 + n % 2)
                    for k in range(TT):
                        tr = pe.transpose(aux[2 + n % 2][:, k * P:(k + 1) * P], prob[:, n % 2, k * P:(k + 1) * P], ident[:])
                    tr.then_inc(aux_steps, 1)

                def values(h):
                    pe.wait_ge(aux_free[2], afree[2].at())
                    pe.wait_ge(aux_free[3], afree[3].at())
                    take_aux(2)
                    for k in range(TT):
                        mm = pe.matmul(aux[2][:], v_tok[:, s, k, h * VH:(h + 1) * VH], PT[:, h, k, :],
                                       start=k == 0, stop=k == TT - 1)
                    mm.then_inc(aux_steps, 1)

                scores(0)
                scores(1)
                next(steps, None)
                for n in range(2 * TT):
                    turn_probs(n)
                    if n + 2 < 2 * TT:
                        scores(n + 2)
                    if n == TT:
                        values(0)
                    elif n < 7:
                        next(steps, None)
                assert next(steps, None) is None
                if ahead:
                    turn_queries()
                values(1)

            for _ in qkv():
                pass
            turn_queries()
            loop = ([(gfree[0], 4), (gfree[1], 4), (gfree[2], 4), (gfree[3], 2), (units, 4)]
                    + [(afree[0], 2), (afree[2], 12), (afree[3], 8), (q_seen, 2), (norm_seen, 16)])
            with turns(pe, PAIRS // 2 - 1, loop):
                for s in range(2):
                    attend(s, True)
            attend(0, True)
            attend(1, False)

            product(xT, KD, True, ready=lambda n: (g_split, n + 1))
            with turns(pe, NB - 1, [(c, 1) for c in gfree] + [(units, 4)]):
                product(xT, KD, True)

            def norm_and_gate(layer):
                pe.wait_ge(p_in, 16 * (layer + 1))
                for f in range(PLE // P):
                    take_aux(f)
                    for t in range(TT):
                        tr = pe.transpose(aux[f][:, t * P:(t + 1) * P], p_tok[:, t, f * P:(f + 1) * P], ident[:])
                    tr.then_inc(aux_steps, 1)
                for t in transpose_tokens():
                    pe.wait_ge(ln_done, layer * TT + t + 1)
                aux_read()
                with turns(pe, NB // 2, [(c, 2) for c in gfree + afree] + [(units, 10)]):
                    for _ in range(2):
                        product(pT, PLE // P, True, banks=aux, take=take_aux)
                        product(xT, KD, True)

            norm_and_gate(0)

            for t in transpose_tokens():
                pe.wait_ge(x_done, TT * NB)
            aux_read()
            slot = units.n % 2
            begin_unit()
            take_gemm(0)
            for k in range(KD):
                mm = passes(gemm[0][:], [w[:, slot, k * 2 * NH:(k + 1) * 2 * NH] for w in W], [x[:, k, :] for x in xT],
                            k == 0, k == KD - 1)
                if k % 4 == 3:
                    mm.then_inc(gemm_steps, 1)

            def turn_dt():
                pe.wait_ge(gemm_free[0], gfree[0].at(-1))
                take_aux(3)
                for t in range(TT):
                    tr = pe.transpose(aux[3][:, t * P:(t + 1) * P], FT[:, t * P:(t + 1) * P], ident[:])
                tr.then_inc(aux_steps, 1)

            def decay_sums():
                pe.wait_ge(dt_step, 2)
                pe.wait_ge(ssd_const, 16 * 5)
                take_aux(0)
                for c in range(TT):
                    for d, tri in enumerate((mask_le, mask_ge)):
                        o = c * 2 * NH + d * NH
                        mm = pe.matmul(aux[0][:, o:o + NH], tri[:], aa[:, c, d * NH:(d + 1) * NH], start=True, stop=True)
                mm.then_inc(aux_steps, 1)
                take_aux(1)
                mm = pe.matmul(aux[1][:], ones[:], aa[:].rearrange("p c n -> p (c n)"), start=True, stop=True)
                mm.then_inc(aux_steps, 1)
                pe.wait_ge(dt_step, 3)
                take_aux(2)
                for c in range(TT):
                    tr = pe.transpose(aux[2][:, c * P:(c + 1) * P], Fs[:, c].rearrange("p d h -> p (d h)"), ident[:])
                tr.then_inc(aux_steps, 1)

            silu, mixed_n, xw, gated = Count(), Count(1), Count(), Count()

            def extras(j, fills, s):
                o = 1 - s
                if j == 0 and any(n[0] == "cb" for _, n, _ in fills):
                    pe.wait_ge(silu_done, silu.at())
                    aux_read()
                for slot_j, (what, n), bank in fills:
                    if slot_j != j:
                        continue
                    if what != "intra" or n % 2 == 0:
                        take_aux(bank)
                    b = aux[bank]
                    if what == "intra":
                        pe.wait_ge(mixed_m, mixed_n.step())
                        c, hf = divmod(n, 2)
                        for h in range(4):
                            cols = slice((4 * hf + h) * HD, (4 * hf + h + 1) * HD)
                            mm = pe.matmul(b[:, cols], MM[n % 2][:, h, :], X[:, o, c, cols], start=True, stop=True)
                    elif what == "cb":
                        for c in range(TT):
                            mm = pe.matmul(b[:, c * P:(c + 1) * P], BT[:, c * P:(c + 1) * P], CT[:, o, c * P:(c + 1) * P],
                                           start=True, stop=True)
                    elif what in ("back", "forth"):
                        pe.wait_ge(xw_done, xw.step())
                        buf = {("back", 3): 0, ("back", 2): 1, ("back", 1): 0}.get((what, n), n % 2)
                        mm = pe.matmul(b[:], Bt[:, o, n, :], Xw[:, buf, :], start=True, stop=True)
                    elif what == "from_f":
                        mm = pe.matmul(b[:], CT[:, o, n * P:(n + 1) * P], st_f[:], start=True, stop=True)
                    elif what == "from_b":
                        if n == 0:
                            pe.wait_ge(aux_free[1], afree[1].at())
                        mm = pe.matmul(b[:], CT[:, o, n * P:(n + 1) * P], st_b[:, n, :], start=True, stop=True)
                    elif what == "ytr":
                        pe.wait_ge(y_gated, gated.step())
                        for f in range(4):
                            mm = pe.transpose(b[:, f * P:(f + 1) * P], yg[:, n % 2, f * P:(f + 1) * P], ident[:])
                    else:
                        pe.wait_ge(silu_done, silu.at(n + 1))
                        src = cv if n < 4 else BT
                        for t in range(TT):
                            mm = pe.transpose(b[:, t * P:(t + 1) * P], src[:, t * P:(t + 1) * P], ident[:])
                    mm.then_inc(aux_steps, 1)

            def group(s, products, ssd, first=False):
                fills = group_fills(products, ssd)
                if products:
                    j = 0
                    for _ in product_units(xT, KD, False):
                        extras(j, fills, s)
                        if first and j == 0:
                            turn_dt()
                        if first and j == 2:
                            decay_sums()
                        j += 1
                    for half in range(2):
                        slot = units.n % 2
                        begin_unit()
                        for i, m in enumerate((2, 3)):
                            if half == 0:
                                take_gemm(m)
                            for k in range(8):
                                kk = 8 * half + k
                                o = k * 2 * NS + i * NS
                                mm = passes(gemm[m][:], [w[:, slot, o:o + NS] for w in W], [x[:, kk, :] for x in xT],
                                            kk == 0, kk == KD - 1)
                                if k % 4 == 3:
                                    mm.then_inc(gemm_steps, 1)
                        extras(j, fills, s)
                        j += 1
                    for _ in product_units(xT, KD, True):
                        extras(j, fills, s)
                        j += 1
                    silu.step(GCH)
                else:
                    for j in range(U_GRP):
                        extras(j, fills, s)
                        if j in Y_SLOTS:
                            next(first_block)
            group(0, True, False, first=True)
            both = group_fills(True, True)
            per = [2 * bank_count(both, m) for m in range(4)]
            with turns(pe, NG // 2 - 1, [(c, n) for c, n in zip(afree, per)] + [(gfree[0], 4), (gfree[1], 4), (gfree[2], 6),
                       (gfree[3], 6), (units, 2 * U_GRP), (silu, 2 * GCH), (mixed_n, 16), (xw, 12), (gated, 8)]):
                group(1, True, True)
                group(0, True, True)
            group(1, True, True)
            first_block = product_units(y_part, 2 * KD, True, order=Y_FIRST, ready=lambda n: (y_lo, 4 * (n + 1)))
            group(0, False, True)

            for _ in first_block:
                pass
            with turns(pe, NB - 1, [(c, 1) for c in gfree] + [(units, 8)]):
                product(y_part, 2 * KD, True, order=Y_ORDER)
            norm_and_gate(1)

        @block.scalar
        def _(act):
            split_unit = Count()
            step0 = Count()
            aux0 = Count()
            order = Count()

            def split():
                s = split_unit.n % 2
                act.wait_ge(gemm_steps, step0.at())
                act.wait_ge(raw_in[s], slot_uses(split_unit))
                act.activation(W[0][:, s, :], raw[:, s, :], ACT.Copy).then_inc(hi_done, 1)
                split_unit.step()

            def next_unit():
                step0.step(4)
                split()

            def split_aux_tokens(t, b):
                act.wait_ge(aux_steps, aux0.step())
                act.activation(xT[0][:, 4 * b:4 * b + 4, t * P:(t + 1) * P],
                               aux[b][:].rearrange("p (k n) -> p k n", k=4), ACT.Copy).then_inc(aux_hi, 1)

            for t in range(TT):
                for b in range(4):
                    split_aux_tokens(t, b)
                if t >= TT - 2:
                    split()
            for j in range(2):
                for u in range(4):
                    next_unit()
                for t in range(TT):
                    act.wait_ge(gemm_free[t], j + 1)
                    if j or t:
                        act.wait_ge(ssq_done, j * TT + t)
                    act.activation(junk[:], c_tok[:, j, t, :], ACT.Square,
                                   accum_out=stat[:, j * TT + t:j * TT + t + 1]).then_inc(ssq_done, 1)
            next_unit()
            act.wait_ge(small_var, 1)
            act.activation(stat[:, 16:24], stat[:, 8:16], ACT.Sqrt).then_inc(small_std, 1)
            act.wait_ge(trig_arg, 2)
            act.activation(sin[:].rearrange("p t n -> p (t n)"), trig[:, 0, :], ACT.Sin).then_inc(trig_done, 1)
            act.activation(cos[:].rearrange("p t n -> p (t n)"), trig[:, 1, :], ACT.Sin).then_inc(trig_done, 1)
            aux0.step()
            with turns(act, NB, [(split_unit, 4), (step0, 16)]) as turn:
                for u in range(4):
                    if u == 3:
                        for m in range(4):
                            act.wait_ge(gemm_steps, step0.at(m + 1))
                            act.activation(zT[:, bass.ds(turn * 4 + m, 1), :].rearrange("p a n -> p (a n)"),
                                           gemm[m][:], ACT.Silu).then_inc(gemm_free[m], 1)
                    next_unit()
            for f in range(2 * KL):
                act.wait_ge(aux_steps, aux0.step())
                act.activation(cT[0][:, f, :], aux[f % 4][:], ACT.Copy, scale=smalls[:, f:f + 1]).then_inc(aux_hi, 1)
            aux0.step()

            maxes = Count()

            def take_qkv(s, step):
                if step < 2:
                    act.wait_ge(gemm_steps, step0.at(step + 1))
                    act.activation(qT[:, s, step, :], gemm[step][:], ACT.Copy).then_inc(gemm_free[step], 1)
                if step == 4:
                    act.wait_ge(gemm_steps, step0.at(2))
                    act.activation(kT[:, s, 1, :], gemm[0][:], ACT.Copy).then_inc(gemm_free[0], 1)
                if step == 6:
                    act.wait_ge(gemm_steps, step0.at(4))
                    act.activation(v_tok[:, s, 2:4, :].rearrange("p t n -> p (t n)"), gemm[2][:], ACT.Copy).then_inc(gemm_free[2], 1)
                if step in (2, 6):
                    next_unit()

            def attend(s, ahead):
                a = {"S": [1, 2, 4, 6, 8, 10, 12, 15], "T": [3, 5, 7, 9, 11, 14, 16, 17]}

                def exp(n):
                    act.wait_ge(max_done, maxes.step())
                    act.wait_ge(aux_steps, aux0.at(a["S"][n]))
                    act.wait_ge(aux_steps, aux0.at(a["T"][n - 2] if n >= 2 else 0))
                    act.activation(prob[:, n % 2, :], aux[n % 2][:], ACT.Exp, bias=stat[:, 40 + n:41 + n], scale=SCALE,
                                   accum_out=stat[:, 48 + n:49 + n]).then_inc(exp_done, 1)

                def take_pt(n):
                    h, t = divmod(n, TT)
                    act.wait_ge(aux_steps, aux0.at(a["T"][n]))
                    act.activation(PT[:, h, :, t * P:(t + 1) * P], aux[2 + n % 2][:].rearrange("p (k n) -> p k n", k=TT),
                                   ACT.Copy).then_inc(aux_free[2 + n % 2], 1)

                exp(0)
                exp(1)
                if ahead:
                    take_qkv(1 - s, 0)
                for n in range(2 * TT):
                    take_pt(n)
                    if n + 2 < 2 * TT:
                        exp(n + 2)
                    if ahead and n - 1 in AHEAD:
                        take_qkv(1 - s, AHEAD[n - 1])
                aux0.step(18 + ahead)

            for step in range(7):
                take_qkv(0, step)
            aux0.step()
            with turns(act, PAIRS // 2 - 1, [(split_unit, 4), (step0, 16), (aux0, 38), (maxes, 16)]):
                for s in range(2):
                    attend(s, True)
            attend(0, True)
            attend(1, False)

            act.wait_ge(aux_free[2], AUX2_ATT)
            for q in range(4):
                act.activation(xT[0][:, 4 * q:4 * q + 4, :].rearrange("p k n -> p (k n)"),
                               g_raw[:, 4 * q:4 * q + 4, :].rearrange("p k n -> p (k n)"), ACT.Copy).then_inc(aux_hi, 1)
            def normalise(layer):
                def centre(t):
                    act.wait_ge(ln_rstd, layer * TT + t + 1)
                    act.activation(xtok[:, t, :], xtok[:, t, :], ACT.Identity, bias=shift[:, t:t + 1],
                                   scale=rvar[:, t:t + 1]).then_inc(ln_centred, 1)

                for t in range(TT):
                    act.wait_ge(small_var, 1 + layer * (TT + 1) + t + 1)
                    act.activation(rstd[:, t:t + 1], rstd[:, t:t + 1], ACT.Sqrt).then_inc(small_std, 1)
                    if t:
                        centre(t - 1)
                for f in range(PLE // P):
                    act.wait_ge(aux_steps, aux0.step())
                    act.activation(pT[0][:, f, :], aux[f][:], ACT.Copy).then_inc(aux_hi, 1)
                centre(TT - 1)

            with turns(act, NB - 1, [(split_unit, 4), (step0, 16)]):
                for u in range(4):
                    next_unit()
            for u in range(3):
                next_unit()
            normalise(0)

            def norm_and_gate(layer):
                for t in range(TT):
                    for b in range(4):
                        split_aux_tokens(t, b)
                    if t == 0:
                        next_unit()
                with turns(act, NB // 2, [(split_unit, 10), (step0, 40)]):
                    for cb in range(2):
                        for u in range(5):
                            if u == 4:
                                for t in range(TT):
                                    act.wait_ge(gemm_steps, step0.at(t + 1))
                                    act.activation(sig[:, t, :], gemm[t][:], ACT.Sigmoid).then_inc(gemm_free[t], 1)
                            next_unit()

            norm_and_gate(0)

            act.wait_ge(x_done, TT * NB)
            act.dma_start(x_mid.rearrange("(t p) n -> p t n", p=P), xtok[:]).then_inc(spill, 16)
            for t in range(TT):
                for b in range(4):
                    split_aux_tokens(t, b)
            act.wait_ge(spill, 16)
            act.wait_ge(pad_zero, 1)
            act.dma_start(ones[:], consts[3]).then_inc(ssd_const, 16)
            act.dma_start(bias_row[:], rows[0:1, 32:160].to_broadcast([P, 2 * NH])).then_inc(ssd_const, 16)
            act.dma_start(alog_row[:], rows[0:1, 160:288].to_broadcast([P, 2 * NH])).then_inc(ssd_const, 16)
            act.dma_start(d_row[:], rows[0:1, 288:352].to_broadcast([P, NH])).then_inc(ssd_const, 16)
            act.dma_start(cw[:], convw).then_inc(ssd_const, 16)
            next_unit()
            act.wait_ge(ssd_const, 16 * 5)
            act.activation(alog_row[:], alog_row[:], ACT.Exp).then_inc(dt_act, 1)
            def decays():
                flat = lambda v: v[:].rearrange("p t d h -> p (t d h)")
                act.wait_ge(dt_step, 3)
                act.activation(flat(eF), flat(Fs), ACT.Exp).then_inc(dt_act, 1)
                act.activation(flat(wst), flat(wst), ACT.Exp).then_inc(dt_act, 1)
                act.activation(flat(eT), flat(eT), ACT.Exp).then_inc(dt_act, 1)
                act.wait_ge(aux_free[2], AUX2_ATT + 2 * TT + NB + 1)
                act.dma_start(f_rows, FT[:]).then_inc(ft_out, 16)
                act.wait_ge(ft_out, 16)
                aux0.step(4)

            sums, convs, gates, outs, mixes = Count(), Count(), Count(), Count(16), Count(1)
            act.sem_inc(y_out, 16)
            act.sem_inc(y_squared, 2)

            def rows_of(q, g):
                c, hf = divmod(q, 2)
                for d in range(2):
                    src = f_rows[bass.ds(g * HG + d * NH + 4 * hf, 4), c * P:(c + 1) * P].unsqueeze(0).to_broadcast([P, 4, P])
                    act.dma_start(FR[:, q % 2, d], src).then_inc(fr_in[q % 2], 16)

            def fetch_y(q):
                act.dma_start(y_raw_quad(q), y_scr[q]).then_inc(y_in[q], 16)

            def scale_y(q):
                act.wait_ge(y_in[q], 16)
                for k in range(4 * q, 4 * q + 4):
                    act.activation(y_part(0, k), y_raw(k), ACT.Copy, scale=smalls[:, 8 + k:9 + k]).then_inc(y_hi, 1)

            def group(s, g, products, ssd, first=False):
                fills = group_fills(products, ssd)
                o = 1 - s
                for j in range(U_GRP):
                    if products:
                        if j == 3:
                            for m in range(4):
                                act.wait_ge(gemm_steps, step0.at(m + 1))
                                act.wait_ge(conv_done, convs.at())
                                act.activation(hp[:, m, PAD:PAD + SEQ], gemm[m][:], ACT.Copy).then_inc(gemm_free[m], 1)
                        if j == 5:
                            act.wait_ge(gemm_steps, step0.at(2))
                            act.wait_ge(conv_done, convs.at(1))
                            act.activation(hp[:, 0, PAD:PAD + SEQ], gemm[2][:], ACT.Copy).then_inc(gemm_free[2], 1)
                        if j == 9:
                            if ssd:
                                act.wait_ge(y_gated, gates.at(1))
                            for t in range(TT):
                                act.wait_ge(gemm_steps, step0.at(t + 1))
                                act.activation(zs[:, t, :], gemm[t][:], ACT.Silu).then_inc(gemm_free[t], 1)
                        next_unit()
                        if first and j == 0:
                            act.wait_ge(dt_step, 1)
                            act.activation(pre[1][:], pre[1][:], ACT.Exp, scale=-1.0).then_inc(dt_act, 1)
                        if first and j == 2:
                            decays()
                    if ssd:
                        if j == 0:
                            act.wait_ge(mixed_m, mixes.at())
                            rows_of(0, g - 1)
                            rows_of(1, g - 1)
                        elif j < 8 and j > 0:
                            if j < 7:
                                act.wait_ge(mixed_m, mixes.step())
                                rows_of(j + 1, g - 1)
                        if not products and j < 4:
                            fetch_y(j)
                        if j < 8:
                            act.wait_ge(summed, sums.step())
                            act.activation(FR[:, j % 2, 0], FR[:, j % 2, 0], ACT.Exp).then_inc(decayed, 1)
                        if j == 7:
                            mixes.step(2)
                        if j in (3, 5, 7, 9):
                            c = (j - 3) // 2
                            act.wait_ge(y_gated, gates.step())
                            act.wait_ge(aux_steps, aux0.at(fill_no(fills, ("ytr", c))))
                            act.wait_ge(y_out, outs.at())
                            act.activation(yTc[:].rearrange("p f n -> p (f n)"), yg[:, c % 2, :], ACT.Square,
                                           accum_out=ssq[:, c, bass.ds(g - 1, 1)]).then_inc(y_squared, 1)
                            act.wait_ge(y_squared, gates.at(2))
                            act.activation(yTc[:].rearrange("p f n -> p (f n)"), aux[0][:], ACT.Copy).then_inc(aux_free[0], 1)
                            act.wait_ge(aux_free[0], free0.at(bank_no(fills, ("ytr", c))))
                            act.dma_start(y_scr[bass.ds(g - 1, 1), :, :, c * P:(c + 1) * P].rearrange("a p f n -> p (a f) n"),
                                          yTc[:]).then_inc(y_out, 16)
                            outs.step(16)
                    if products and j >= 4:
                        n = j - 4
                        if n >= 1:
                            act.wait_ge(aux_steps, aux0.at(fill_no(fills, ("ctr", n - 1))))
                            bank = 2 if j % 2 else 0
                            dst = X[:, s, :, (n - 1) * P:n * P] if n <= 4 else Bt[:, s]
                            act.activation(dst, aux[bank][:].rearrange("p (t n) -> p t n", t=TT), ACT.Copy)\
                               .then_inc(aux_free[bank], 1)
                        act.wait_ge(conv_done, convs.at(n + 1))
                        dst = cv[:] if n < 4 else BT[:] if n == 4 else CT[:, s, :]
                        act.activation(dst, cv[:], ACT.Silu).then_inc(silu_done, 1)
                        if j == 5:
                            act.wait_ge(gemm_steps, step0.at(0))
                            act.activation(hp[:, 1, PAD:PAD + SEQ], gemm[3][:], ACT.Copy).then_inc(gemm_free[3], 1)
                    if not products and j in Y_STEPS:
                        scale_y(Y_STEPS[j])
                    if not products and j in (3, 5, 7):
                        next_unit()
                if products:
                    convs.step(GCH)
                aux0.step(len(fills))
                free0.step(bank_count(fills, 0))

            free0 = Count(AUX0_SSD)
            group(0, 0, True, False, first=True)
            both = group_fills(True, True)
            with turns(act, NG // 2 - 1, [(split_unit, 2 * U_GRP), (step0, 8 * U_GRP), (aux0, 2 * len(both)),
                       (free0, 2 * bank_count(both, 0)), (convs, 2 * GCH), (sums, 16), (mixes, 16), (gates, 8), (outs, 128)]) as turn:
                group(1, turn * 2 + 1, True, True)
                group(0, turn * 2 + 2, True, True)
            group(1, NG - 1, True, True)
            group(0, NG, False, True)

            act.wait_ge(y_out, outs.at())
            for q in (7, 4, 5, 6):
                fetch_y(q)
            act.dma_start(xtok[:, :, 0:D - BLK], x_mid.rearrange("(t p) n -> p t n", p=P)[:, :, 0:D - BLK]).then_inc(resid1, 16)
            act.wait_ge(small_var, TT + 2)
            act.activation(stat[:, 104:108], stat[:, 100:104], ACT.Sqrt).then_inc(small_std, 1)
            for q, units in ((7, 1), (4, 0), (5, 1), (6, 3)):
                scale_y(q)
                for u in range(units):
                    next_unit()
            with turns(act, NB - 2, [(split_unit, 8), (step0, 32)]):
                for u in range(8):
                    next_unit()
            for u in range(7):
                next_unit()
                if u == 0:
                    act.dma_start(xtok[:, :, D - BLK:], x_mid.rearrange("(t p) n -> p t n", p=P)[:, :, D - BLK:]).then_inc(resid1, 16)
            normalise(1)
            norm_and_gate(1)

        @block.vector
        def _(dve):
            split_unit, step0, aux0, hi = Count(), Count(), Count(), Count()
            gfree = [Count() for _ in range(4)]
            afree = [Count() for _ in range(4)]
            order = Count()

            def link(ins):
                ins.then_inc(dve_order, 1)
                dve.wait_ge(dve_order, order.step())

            def split():
                s = split_unit.n % 2
                dve.wait_ge(hi_done, split_unit.at(1))
                dve.tensor_tensor(W[1][:, s, :], raw[:, s, :], W[0][:, s, :].bitcast(F32), ALU.subtract)\
                   .then_inc(split_done, 1)
                split_unit.step()

            def next_unit():
                step0.step(4)
                split()

            def freed(ins, which, counts, m):
                ins.then_inc(which[m], 1)
                counts[m].step()

            def split_aux_tokens(t, b):
                aux0.step()
                dve.wait_ge(aux_hi, hi.step())
                dst = slice(t * P, (t + 1) * P)
                freed(dve.tensor_tensor(xT[1][:, 4 * b:4 * b + 4, dst], aux[b][:].rearrange("p (k n) -> p k n", k=4),
                                        xT[0][:, 4 * b:4 * b + 4, dst].bitcast(F32), ALU.subtract), aux_free, afree, b)

            dve.wait_ge(const_in, 16 * 6)
            link(dve.tensor_copy(pos_f[:], pos_i[:]))
            for t in range(TT):
                ins = dve.tensor_scalar(trig[:, 2, t * 32:(t + 1) * 32], invf[:], pos_f[:, t:t + 1], None, ALU.mult)
            link(ins)
            for n, quarter in enumerate((0.0, 0.25)):
                k, r = trig[:, 3, :], trig[:, n, :]
                link(dve.tensor_scalar(k, trig[:, 2, :], float(1 / (2 * np.pi)), quarter, ALU.mult, ALU.add))
                link(dve.tensor_scalar(k, k, ROUND, None, ALU.add))
                link(dve.tensor_scalar(k, k, -ROUND, None, ALU.add))
                link(dve.scalar_tensor_tensor(r, k, -TWO_PI_PARTS[0], trig[:, 2, :], ALU.mult, ALU.add))
                link(dve.scalar_tensor_tensor(r, k, -TWO_PI_PARTS[1], r, ALU.mult, ALU.add))
                link(dve.scalar_tensor_tensor(r, k, -TWO_PI_PARTS[2], r, ALU.mult, ALU.add))
                link(dve.tensor_scalar(r, r, float(2 * np.pi * quarter), PI32, ALU.add, ALU.min))
                dve.tensor_scalar(r, r, -PI32, None, ALU.max).then_inc(trig_arg, 1)

            for t in range(TT):
                for b in range(4):
                    split_aux_tokens(t, b)
                if t >= TT - 2:
                    split()
            for j in range(2):
                for u in range(4):
                    if u == 3:
                        for t in range(TT):
                            dve.wait_ge(gemm_steps, step0.at(t + 1))
                            freed(dve.tensor_copy(c_tok[:, j, t, :], gemm[t][:]), gemm_free, gfree, t)
                    next_unit()
            dve.wait_ge(gemm_steps, step0.at(4))
            dve.wait_ge(ssq_done, 2 * TT)
            freed(dve.tensor_copy(kF[0:ROPE, :], gemm[0][0:ROPE, :]), gemm_free, gfree, 0)
            next_unit()
            dve.wait_ge(aux_steps, aux0.step())
            freed(dve.tensor_copy(k_tok[:].rearrange("p t n -> p (t n)"), aux[0][:, 0:TT * ROPE]), aux_free, afree, 0)
            dve.wait_ge(ssq_done, 2 * TT)
            dve.tensor_scalar(stat[:, 8:16], stat[:, 0:8], 1.0 / LORA, RMS_EPS, ALU.mult, ALU.add).then_inc(small_var, 1)
            dve.wait_ge(small_std, 1)
            link(dve.reciprocal(stat[:, 24:32], stat[:, 16:24]))
            for j in range(2):
                for t in range(TT):
                    dve.tensor_scalar(c_tok[:, j, t, :], c_tok[:, j, t, :], stat[:, 24 + j * TT + t:25 + j * TT + t],
                                      None, ALU.mult).then_inc(c_normed, 1)
            with turns(dve, NB, [(split_unit, 4), (step0, 16)] + [(c, 1) for c in gfree]):
                for u in range(4):
                    next_unit()
                for c in gfree:
                    c.step()
            for f in range(2 * KL):
                aux0.step()
                dve.wait_ge(aux_hi, hi.step())
                freed(dve.scalar_tensor_tensor(cT[1][:, f, :], aux[f % 4][:], smalls[:, f:f + 1],
                                               cT[0][:, f, :].bitcast(F32), ALU.mult, ALU.subtract), aux_free, afree, f % 4)
            dve.wait_ge(aux_steps, aux0.step())
            freed(dve.tensor_copy(krT[:], aux[0][:]), aux_free, afree, 0)

            exps, pairs = Count(), Count(1)

            def take_qkv(s, step):
                if step == 2:
                    dve.wait_ge(gemm_steps, step0.at(4))
                    dve.wait_ge(q_rotated, pairs.at())
                    dve.tensor_copy(q_tok[:].rearrange("p t h a b -> p (t h a b)"), gemm[2][:]).then_inc(gemm_free[2], 1)
                    pairs.step()
                if step == 3:
                    dve.wait_ge(gemm_steps, step0.at(4 + 1))
                    dve.tensor_copy(kT[:, s, 0, :], gemm[3][:]).then_inc(gemm_free[3], 1)
                if step == 5:
                    dve.wait_ge(gemm_steps, step0.at(3))
                    dve.tensor_copy(v_tok[:, s, 0:2, :].rearrange("p t n -> p (t n)"), gemm[1][:]).then_inc(gemm_free[1], 1)
                if step == 6:
                    gfree[0].step(2), gfree[1].step(2), gfree[2].step(2), gfree[3].step(1)

            def take_queries(s, fill):
                dve.wait_ge(aux_steps, aux0.at(fill))
                freed(dve.tensor_copy(qrT[:, s, :], aux[0][:]), aux_free, afree, 0)

            def attend(s, pair, ahead=True):
                a_s = [1, 2, 4, 6, 8, 10, 12, 15]

                def top(n):
                    dve.wait_ge(aux_steps, aux0.at(a_s[n]))
                    link(dve.tensor_reduce(stat[:, 32 + n:33 + n], aux[n % 2][:], AX.X, ALU.max))
                    dve.tensor_scalar(stat[:, 40 + n:41 + n], stat[:, 32 + n:33 + n], -SCALE, None, ALU.mult).then_inc(max_done, 1)

                def normalise(n):
                    dve.wait_ge(exp_done, exps.step())
                    link(dve.reciprocal(stat[:, 56 + n:57 + n], stat[:, 48 + n:49 + n]))
                    dve.tensor_scalar(prob[:, n % 2, :], prob[:, n % 2, :], stat[:, 56 + n:57 + n], None,
                                      ALU.mult).then_inc(norm_done, 1)

                def gate(h, fill):
                    dve.wait_ge(aux_steps, aux0.at(fill))
                    g = (pair * 2 + h)
                    dve.tensor_tensor(g_raw[:, bass.ds(g, 1), :].rearrange("p a n -> p (a n)"), aux[2][:],
                                      zT[:, bass.ds(g, 1), :].rearrange("p a n -> p (a n)"), ALU.mult).then_inc(aux_free[2], 1)

                top(0)
                top(1)
                for n in range(2 * TT):
                    normalise(n)
                    if n + 2 < 2 * TT:
                        top(n + 2)
                    if n == 5:
                        gate(0, 13)
                    if n == (1 if ahead else 7) or ahead and n == 4:
                        next_unit()
                    if ahead and n - 1 in AHEAD:
                        take_qkv(1 - s, AHEAD[n - 1])
                if ahead:
                    take_queries(1 - s, 18)
                gate(1, 18 + ahead)
                aux0.step(18 + ahead)
                afree[2].step(6), afree[3].step(4)

            for step in range(7):
                take_qkv(0, step)
                if step == 3:
                    next_unit()
            take_queries(0, 1)
            aux0.step()
            with turns(dve, PAIRS // 2 - 1, [(split_unit, 4), (step0, 16), (aux0, 38), (order, 32), (exps, 16), (pairs, 2)]
                       + [(gfree[0], 4), (gfree[1], 4), (gfree[2], 4), (gfree[3], 2), (afree[0], 2), (afree[2], 12), (afree[3], 8)]) as turn:
                for s in range(2):
                    attend(s, turn * 2 + s)
            attend(0, PAIRS - 2)
            attend(1, PAIRS - 1, False)

            for q in range(4):
                dve.wait_ge(aux_hi, hi.step())
                a = slice(4 * q, 4 * q + 4)
                dve.tensor_tensor(xT[1][:, a, :], g_raw[:, a, :], xT[0][:, a, :].bitcast(F32), ALU.subtract).then_inc(g_split, 1)

            def mix(layer, cb, t):
                xb = xtok[:, t, bass.ds(cb * BLK, BLK)]
                dve.wait_ge(gemm_steps, step0.at(t + 1))
                if layer == 0:
                    ins = dve.scalar_tensor_tensor(xb, xb, ALPHA, gemm[t][:], ALU.mult, ALU.add)
                else:
                    ins = dve.scalar_tensor_tensor(xb, gemm[t][:], stat[:, 108 + t:109 + t], xb, ALU.mult, ALU.add)
                freed(ins, gemm_free, gfree, t)
                dve.wait_ge(gemm_free[t], gfree[t].at())
                dve.bn_stats(bstat[:, t, bass.ds(cb, 1), :].rearrange("p a n -> p (a n)"), xb).then_inc(ln_stat, 1)
                stats.step()

            def last_block(layer, units_of_block):
                def scales(t):
                    dve.wait_ge(small_std, 1 + layer * (TT + 1) + t + 1)
                    link(dve.reciprocal(rvar[:, t:t + 1], rstd[:, t:t + 1]))
                    dve.scalar_tensor_tensor(shift[:, t:t + 1], bmean[:, t, 0:1], -1.0, rvar[:, t:t + 1],
                                             ALU.mult, ALU.mult).then_inc(ln_rstd, 1)

                def times_g(t):
                    dve.wait_ge(ln_centred, layer * TT + t + 1)
                    dve.tensor_tensor(xtok[:, t, :], xtok[:, t, :], ln_g[:], ALU.mult).then_inc(ln_scaled, 1)

                for u in range(units_of_block - 1):
                    next_unit()
                dve.wait_ge(ln_in, 32 * (layer + 1))
                for t in range(TT):
                    mix(layer, NB - 1, t)
                    dve.wait_ge(ln_stat, stats.at())
                    link(dve.bn_aggr(bmean[:, t, :], bstat[:, t].rearrange("p a n -> p (a n)")))
                    dve.tensor_scalar(rstd[:, t:t + 1], bmean[:, t, 1:2], LN_EPS, None, ALU.add).then_inc(small_var, 1)
                    if t > 0:
                        scales(t - 1)
                    if t > 1:
                        times_g(t - 2)
                scales(TT - 1)
                for f in range(PLE // P):
                    aux0.step()
                    dve.wait_ge(aux_hi, hi.step())
                    freed(dve.tensor_tensor(pT[1][:, f, :], aux[f][:], pT[0][:, f, :].bitcast(F32), ALU.subtract),
                          aux_free, afree, f)
                times_g(TT - 2)
                times_g(TT - 1)

            def mixed(layer, n_blocks, first, units_of_block):
                def block(cb):
                    for u in range(units_of_block):
                        if u == units_of_block - 1:
                            for t in range(TT):
                                mix(layer, cb, t)
                        next_unit()

                if n_blocks > 1:
                    with turns(dve, n_blocks, [(split_unit, units_of_block), (step0, 4 * units_of_block), (stats, TT)]
                               + [(c, 1) for c in gfree]) as turn:
                        block(turn + first if first else turn)
                else:
                    block(first)

            stats = Count()

            def norm_and_gate(layer):
                for t in range(TT):
                    for b in range(4):
                        split_aux_tokens(t, b)
                    if t == 0:
                        next_unit()
                with turns(dve, NB // 2, [(split_unit, 10), (step0, 40)] + [(c, 2) for c in gfree + afree]) as turn:
                    for cb in range(2):
                        for u in range(5):
                            if u == 4:
                                for t in range(TT):
                                    gfree[t].step()
                                    dve.wait_ge(gemm_free[t], gfree[t].at())
                                    freed(dve.tensor_tensor(pe_g[:, t, :], aux[t][:], sig[:, t, :], ALU.mult), aux_free, afree, t)
                                    dve.wait_ge(aux_free[t], afree[t].at())
                                    xb = xtok[:, t, bass.ds(turn * 2 * BLK + cb * BLK, BLK)]
                                    dve.tensor_tensor(xb, xb, pe_g[:, t, :], ALU.add).then_inc(x_done, 1)
                            next_unit()

            dve.wait_ge(resid, 16)
            mixed(0, NB - 1, 0, 4)
            last_block(0, 4)
            norm_and_gate(0)

            for t in range(TT):
                for b in range(4):
                    split_aux_tokens(t, b)
            dve.memset(hp[:], 0.0).then_inc(pad_zero, 1)
            dve.wait_ge(ssd_const, 16 * 5)
            dve.wait_ge(gemm_steps, step0.at(4))
            freed(dve.tensor_copy(FT[:], gemm[0][:]), gemm_free, gfree, 0)
            next_unit()
            dve.wait_ge(aux_steps, aux0.step())
            freed(dve.tensor_tensor(pre[0][:], aux[3][:].rearrange("p (t n) -> p t n", t=TT),
                                    bias_row[:].unsqueeze(1).to_broadcast([P, TT, 2 * NH]), ALU.add), aux_free, afree, 3)
            dve.wait_ge(aux_free[3], afree[3].at())
            dve.scalar_tensor_tensor(pre[1][:], pre[0][:], -1.0, pre[0][:], ALU.mult, ALU.max).then_inc(dt_step, 1)
            dve.wait_ge(dt_act, 2)
            link(dve.tensor_scalar(pre[2][:], pre[1][:], 2.0, None, ALU.add))
            link(dve.reciprocal(pre[3][:], pre[2][:]))
            link(dve.tensor_tensor(pre[2][:], pre[1][:], pre[3][:], ALU.mult))
            link(dve.tensor_tensor(pre[3][:], pre[2][:], pre[2][:], ALU.mult))
            acc = dt[:].rearrange("p t d h -> p t (d h)")
            link(dve.tensor_scalar(acc, pre[3][:], 1 / 15, None, ALU.mult))
            for k in (13, 11, 9, 7, 5, 3):
                link(dve.scalar_tensor_tensor(acc, acc, 1 / k, pre[3][:], ALU.add, ALU.mult))
            link(dve.scalar_tensor_tensor(acc, acc, 1.0, pre[2][:], ALU.add, ALU.mult))
            link(dve.tensor_scalar(pre[1][:], pre[0][:], 0.0, None, ALU.max))
            link(dve.scalar_tensor_tensor(acc, acc, 2.0, pre[1][:], ALU.mult, ALU.add))
            dve.scalar_tensor_tensor(aa[:], acc, -1.0, alog_row[:].unsqueeze(1).to_broadcast([P, TT, 2 * NH]),
                                     ALU.mult, ALU.mult).then_inc(dt_step, 1)
            flat = lambda v: v[:].rearrange("p t d h -> p (t d h)")
            dve.wait_ge(aux_steps, aux0.step())
            freed(dve.tensor_copy(flat(Fs), aux[0][:]), aux_free, afree, 0)
            dve.wait_ge(aux_steps, aux0.step())
            freed(dve.tensor_copy(flat(eT), aux[1][:]), aux_free, afree, 1)
            for b in range(2):
                dve.wait_ge(aux_free[b], afree[b].at())
            dve.tensor_tensor(flat(wst), flat(eT), flat(Fs), ALU.subtract).then_inc(dt_step, 1)
            dve.wait_ge(aux_steps, aux0.step())
            freed(dve.tensor_copy(FT[:], aux[2][:]), aux_free, afree, 2)
            dve.wait_ge(dt_act, 5)
            link(dve.tensor_tensor(flat(wst), flat(wst), flat(dt), ALU.mult))

            convs, xds, frs, silus, halves = Count(), Count(), [Count(), Count()], Count(), Count(1)
            dve.sem_inc(weighted, 1)

            def per_head(v):
                return v.unsqueeze(2).to_broadcast([P, HG, HD])

            def heads(v):
                return v.rearrange("p (h n) -> p h n", h=HG)

            def convolve(n, fills):
                src = hp[:, n % 4, :]
                w = lambda k: g_cw[:, n, k:k + 1]
                if n == 0 or n == 5:
                    dve.wait_ge(silu_done, silus.at(n))
                else:
                    dve.wait_ge(aux_steps, aux0.at(fill_no(fills, ("ctr", n - 1))))
                link(dve.tensor_scalar(cv[:], src[:, 0:SEQ], w(0), w(TAPS), ALU.mult, ALU.add))
                for k in range(1, TAPS):
                    ins = dve.scalar_tensor_tensor(cv[:], src[:, k:k + SEQ], w(k), cv[:], ALU.mult, ALU.add)
                    if k < TAPS - 1:
                        link(ins)
                ins.then_inc(conv_done, 1)
                convs.step()

            def half(q, fills):
                c, hf = divmod(q, 2)
                if q == 0:
                    dve.wait_ge(aux_steps, aux0.at(fill_no(fills, ("cb", 0))))
                    dve.tensor_copy(CB[:].rearrange("p c n -> p (c n)"), aux[0][:]).then_inc(aux_free[0], 1)
                    dve.wait_ge(aux_free[0], base0.at(bank_no(fills, ("cb", 0))))
                if hf == 0:
                    dve.wait_ge(weighted, halves.at())
                    dve.tensor_tensor(CBU[:], CB[:, c, :], mask_le[:], ALU.mult)
                    link(dve.tensor_tensor(CBL[:], CB[:, c, :], mask_ge[:], ALU.mult))
                dve.wait_ge(fr_in[q % 2], frs[q % 2].step(32))
                for d in range(2):
                    for h in range(4):
                        e = FR[:, q % 2, d, h, :]
                        hh = 4 * hf + h
                        ins = dve.tensor_scalar(e, e, g_F[:, c, d, hh:hh + 1], 0.0, ALU.subtract, ALU.min)
                ins.then_inc(clipped, 1)
                dve.wait_ge(aux_steps, aux0.at(fill_no(fills, ("intra", q - 2)) if q > 1 else 0))
                M = MM[q % 2]
                for h in range(4):
                    hh = 4 * hf + h
                    ins = dve.tensor_scalar(M[:, h, :], CBL[:], g_dt[:, c, 1, hh:hh + 1], None, ALU.mult)
                link(ins)
                for h in range(4):
                    hh = 4 * hf + h
                    ins = dve.scalar_tensor_tensor(M[:, h, :], CBU[:], g_dt[:, c, 0, hh:hh + 1], M[:, h, :], ALU.mult, ALU.add)
                ins.then_inc(weighted, 1)
                halves.step()

            def state(kind, c, fills):
                bank = 2 if (kind, c) == ("back", 2) else 1
                dve.wait_ge(aux_steps, aux0.at(fill_no(fills, (kind, c))))
                for b in (1, 2):
                    dve.wait_ge(aux_free[b], base12[b].at(seen(fills, b, kind, c)))
                first = (kind, c) in (("back", 3), ("forth", 0))
                dst = st_f[:] if kind == "forth" else st_b[:, c - 1, :]
                src = st_f[:] if kind == "forth" else st_b[:, min(c, 2), :]
                if first:
                    dve.tensor_copy(dst, aux[bank][:]).then_inc(aux_free[bank], 1)
                else:
                    d = 0 if kind == "forth" else 1
                    link(dve.tensor_tensor(heads(dst), heads(src), per_head(g_tot[:, c, d, :]), ALU.mult))
                    dve.tensor_tensor(dst, dst, aux[bank][:], ALU.add).then_inc(aux_free[bank], 1)

            def seen(fills, bank, kind, c):
                at = fill_no(fills, (kind, c)) - 1
                return sum(b == bank and not second_half(n) for _, n, b in fills[:at])

            def assemble(c, fills):
                y = yg[:, c % 2, :]
                dve.wait_ge(xd_done, xds.step())
                for d, name, bank in ((0, "from_f", 1), (1, "from_b", 2)):
                    if (name, c) not in [n for _, n, _ in fills]:
                        continue
                    dve.wait_ge(aux_steps, aux0.at(fill_no(fills, (name, c))))
                    dve.tensor_tensor(heads(uu[:]), heads(aux[bank][:]), per_head(g_e[:, c, d, :]), ALU.mult).then_inc(aux_free[bank], 1)
                    dve.wait_ge(aux_free[bank], base12[bank].at(bank_no(fills, (name, c))))
                    link(dve.tensor_tensor(y, y, uu[:], ALU.add))
                dve.wait_ge(aux_steps, aux0.at(fill_no(fills, ("intra", 2 * c + 1))))
                dve.tensor_tensor(y, y, aux[3][:], ALU.add).then_inc(aux_free[3], 1)
                dve.wait_ge(aux_free[3], base3.at(c + 1))
                dve.tensor_tensor(y, y, zs[:, c, :], ALU.mult).then_inc(y_gated, 1)

            def split_y(q):
                for k in range(4 * q, 4 * q + 4):
                    dve.wait_ge(y_hi, yhi.step())
                    dve.scalar_tensor_tensor(y_part(1, k), y_raw(k), smalls[:, 8 + k:9 + k], y_part(0, k).bitcast(F32),
                                             ALU.mult, ALU.subtract).then_inc(y_lo, 1)

            def group(g, products, ssd):
                fills = group_fills(products, ssd)
                for j in range(U_GRP):
                    if ssd and j == 0:
                        dve.wait_ge(gemm_free[3], gbase[3].at())
                        for dst, src in ((g_F, Fs), (g_dt, dt), (g_w, wst), (g_e, eF), (g_tot, eT)):
                            dve.tensor_copy(dst[:], src[:, :, :, bass.ds((g - 1) * HG, HG)])
                        dve.tensor_copy(g_d[:], d_row[:, bass.ds((g - 1) * HG, HG)]).then_inc(group_scal, 1)
                        dve.wait_ge(group_scal, scal.step())
                        half(0, fills)
                        state("back", 3, fills)
                        state("back", 2, fills)
                    if products:
                        if j == 3:
                            dve.tensor_copy(g_cw[:, 0:4, :], cw[:, bass.ds(g * 4, 4), :])
                            dve.tensor_copy(g_cw[:, 4:5, :], cw[:, bass.ds(g + DI // P, 1), :])
                            link(dve.tensor_copy(g_cw[:, 5:6, :], cw[:, bass.ds(g + DI // P + NG, 1), :]))
                        if j >= 4:
                            n = j - 4
                            m = n if n < 4 else n - 2
                            dve.wait_ge(gemm_free[m], gbase[m].at(2 if n >= 4 else 1))
                            convolve(n, fills)
                    if ssd:
                        if j == 1:
                            state("back", 1, fills)
                        if j in (3, 5, 7):
                            state("forth", (j - 3) // 2, fills)
                        if j in (2, 4, 6, 8):
                            assemble((j - 2) // 2, fills)
                        if j < 7:
                            half(j + 1, fills)
                        if not products and j in Y_STEPS:
                            split_y(Y_STEPS[j])
                if products:
                    for m in range(4):
                        gbase[m].step(2 + (m >= 2))
                    silus.step(GCH)
                aux0.step(len(fills))
                base0.step(bank_count(fills, 0))
                base12[1].step(bank_count(fills, 1))
                base12[2].step(bank_count(fills, 2))
                base3.step(bank_count(fills, 3))

            scal = Count()
            gbase = gfree
            base0, base3, base12 = Count(afree[0].n), Count(afree[3].n), {b: Count(afree[b].n) for b in (1, 2)}
            both = group_fills(True, True)
            group(0, True, False)
            with turns(dve, NG // 2 - 1, [(aux0, 2 * len(both)),
                       (base0, 2 * bank_count(both, 0)), (base3, 2 * bank_count(both, 3)),
                       (base12[1], 2 * bank_count(both, 1)), (base12[2], 2 * bank_count(both, 2)), (convs, 2 * GCH),
                       (silus, 2 * GCH), (xds, 8), (scal, 2), (halves, 16), (frs[0], 256), (frs[1], 256), (order, ORDER_2)]
                       + [(gbase[m], 4 + 2 * (m >= 2)) for m in range(4)]) as turn:
                group(turn * 2 + 1, True, True)
                group(turn * 2 + 2, True, True)
            group(NG - 1, True, True)
            yhi = Count()
            group(NG, False, True)
            split_unit.step(NG * U_GRP + 3)
            step0.step(4 * (NG * U_GRP + 3))
            dve.wait_ge(split_done, split_unit.at())
            for b, c in ((0, base0), (1, base12[1]), (2, base12[2]), (3, base3)):
                afree[b].n = c.n

            dve.wait_ge(y_squared, NG * TT + 2)
            link(dve.tensor_reduce(stat[:, 96:100], ssq, AX.X, ALU.add))
            dve.tensor_scalar(stat[:, 100:104], stat[:, 96:100], 1.0 / DI, RMS_EPS, ALU.mult, ALU.add).then_inc(small_var, 1)
            dve.wait_ge(small_std, TT + 2)
            link(dve.reciprocal(stat[:, 108:112], stat[:, 104:108]))
            for q, units in ((7, 1), (4, 0), (5, 1), (6, 2)):
                split_y(q)
                for u in range(units):
                    next_unit()
            dve.wait_ge(alpha_done, 1)
            mixed(1, 1, 0, 1)
            mixed(1, NB - 2, 1, 8)
            dve.wait_ge(alpha_done, 2)
            last_block(1, 8)
            norm_and_gate(1)

        @block.gpsimd
        def _(pool):
            order = Count()

            def link(ins):
                ins.then_inc(pool_order, 1)
                pool.wait_ge(pool_order, order.step())

            def rotate(dst, src, c, s, a, b, done):
                pool.tensor_tensor(a, src[0], c, ALU.mult)
                link(pool.tensor_tensor(b, src[1], s, ALU.mult))
                link(pool.tensor_tensor(dst[0], a, b, ALU.subtract))
                pool.tensor_tensor(a, src[1], c, ALU.mult)
                link(pool.tensor_tensor(b, src[0], s, ALU.mult))
                pool.tensor_tensor(dst[1], a, b, ALU.add).then_inc(done, 1)

            pool.sem_inc(q_rotated, 1)
            pool.sem_inc(mixed_m, 1)
            pool.wait_ge(trig_done, 2)
            pool.wait_ge(aux_free[0], TT + 1)
            for copy in range(2):
                if copy:
                    pool.wait_ge(k_rotated, copy)
                h = ROPE // 2
                rotate([k_rot[:, :, copy, 0:h], k_rot[:, :, copy, h:]], [k_tok[:, :, 0:h], k_tok[:, :, h:]],
                       cos[:], sin[:], rk_a[:], rk_b[:], k_rotated)
            pairs = Count(1)
            cb = cos[:].unsqueeze(2).to_broadcast([P, TT, 2, ROPE // 2])
            sb_ = sin[:].unsqueeze(2).to_broadcast([P, TT, 2, ROPE // 2])
            turned = Count(TT + 1 + 2 + 1)
            g2 = Count(6)
            with turns(pool, PAIRS, [(order, 3), (pairs, 1), (turned, 1), (g2, 2)]):
                pool.wait_ge(gemm_free[2], g2.at(1))
                pool.wait_ge(q_rotated, pairs.at())
                pool.wait_ge(aux_free[0], turned.at())
                rotate([q_rot[:, :, :, 0, :], q_rot[:, :, :, 1, :]], [q_tok[:, :, :, 0, :], q_tok[:, :, :, 1, :]],
                       cb, sb_, rope_a[:], rope_b[:], q_rotated)
                pairs.step(), turned.step(), g2.step(2)

            def shift(layer):
                pool.wait_ge(ln_in, 32 * (layer + 1))
                for t in range(TT):
                    pool.wait_ge(ln_scaled, layer * TT + t + 1)
                    pool.tensor_tensor(xtok[:, t, :], xtok[:, t, :], ln_b[:], ALU.add).then_inc(ln_done, 1)

            shift(0)

            def per_head(v):
                return v.unsqueeze(2).to_broadcast([P, HG, HD])

            def heads(v):
                return v.rearrange("p (h n) -> p h n", h=HG)

            scal, silus, clips, muls, squares = Count(), Count(), Count(), Count(1), Count()
            aux0 = Count(AUX_SSD)

            def weigh(o, c, d, buf):
                pool.tensor_tensor(heads(Xw[:, buf, :]), heads(X[:, o, c, :]), per_head(g_w[:, c, d, :]), ALU.mult).then_inc(xw_done, 1)

            def next_unit():
                slot = split_unit.n % 2
                pool.wait_ge(hi_done, split_unit.at(1))
                pool.tensor_tensor(W[1][:, slot, :], raw[:, slot, :], W[0][:, slot, :].bitcast(F32), ALU.subtract)\
                    .then_inc(split_done, 1)
                split_unit.step()

            def add_exponents(q):
                pool.wait_ge(clipped, clips.step())
                pool.tensor_tensor(FR[:, q % 2, 0], FR[:, q % 2, 0], FR[:, q % 2, 1], ALU.add).then_inc(summed, 1)

            def group(s, products, ssd):
                o = 1 - s
                fills = group_fills(products, ssd)
                if ssd:
                    pool.wait_ge(group_scal, scal.step())
                    pool.wait_ge(silu_done, silus.step(GCH))
                    weigh(o, 3, 1, 0)
                    weigh(o, 2, 1, 1)
                for j in range(U_GRP):
                    if ssd and j == 1:
                        pool.wait_ge(aux_steps, aux0.at(fill_no(fills, ("back", 3))))
                        weigh(o, 1, 1, 0)
                    if products:
                        next_unit()
                    if not ssd or j >= 8:
                        continue
                    if j == 0:
                        add_exponents(0)
                    pool.wait_ge(decayed, muls.at())
                    pool.wait_ge(weighted, muls.at(1))
                    pool.tensor_tensor(MM[j % 2][:], MM[j % 2][:], FR[:, j % 2, 0], ALU.mult).then_inc(mixed_m, 1)
                    muls.step()
                    if j in (2, 4, 6):
                        c = (j - 2) // 2
                        before = [("back", 1), ("back", 2), ("forth", 0)][c]
                        pool.wait_ge(aux_steps, aux0.at(fill_no(fills, before)))
                        weigh(o, c, 0, c % 2)
                    if j in (0, 3, 5, 7):
                        c = j // 2
                        pool.wait_ge(y_squared, squares.at(1))
                        pool.tensor_tensor(heads(yg[:, c % 2, :]), heads(X[:, o, c, :]), per_head(g_d[:]), ALU.mult).then_inc(xd_done, 1)
                        squares.step()
                    if j < 7:
                        add_exponents(j + 1)
                    if not products and j in (3, 5, 7):
                        next_unit()
                aux0.step(len(fills))

            both = group_fills(True, True)
            split_unit = Count(UNITS - U_GATE - U_OUT - NG * U_GRP + 2)
            pool.wait_ge(split_done, split_unit.at())
            group(0, True, False)
            with turns(pool, NG // 2 - 1, [(scal, 2), (silus, 2 * GCH), (clips, 16), (muls, 16), (squares, 8),
                       (split_unit, 2 * U_GRP), (aux0, 2 * len(both))]):
                group(1, True, True)
                group(0, True, True)
            group(1, True, True)
            group(0, False, True)
            for n in range(2):
                pool.wait_ge(resid1, 16 * (n + 1))
                cols = slice(0, D - BLK) if n == 0 else slice(D - BLK, D)
                pool.tensor_scalar(xtok[:, :, cols], xtok[:, :, cols], ALPHA, 1.0, ALU.mult, ALU.mult).then_inc(alpha_done, 1)
            shift(1)


def layout(inputs):
    f = lambda n: np.asarray(inputs[n])
    units = []

    def add(w, k_tiles, cols):
        per = max(1, UNIT // cols)
        w = w.reshape(k_tiles, P, cols)
        for k in range(0, k_tiles, per):
            u = w[k:k + per].transpose(1, 0, 2).reshape(P, -1)
            if u.shape[1] < UNIT:
                u = np.concatenate([u, np.zeros((P, UNIT - u.shape[1]), u.dtype)], 1)
            units.append(u)

    def blocks(w, n=BLK):
        for c in range(0, w.shape[1], n):
            add(w[:, c:c + n], w.shape[0] // P, n)

    def gate(layer):
        for c in range(0, D, BLK):
            add(f("ple_w_proj")[layer][:, c:c + BLK], PLE // P, BLK)
            add(f("ple_w_gate")[layer][:, c:c + BLK], KD, BLK)

    w = f("mla_w_in")[0]
    blocks(w[:, 0:2 * LORA])
    add(w[:, 2 * LORA:2 * LORA + ROPE], KD, ROPE)
    blocks(w[:, 2 * LORA + ROPE:])
    for g in range(PAIRS):
        u = f("mla_w_uq")[0][:, g * 2 * QKH:(g + 1) * 2 * QKH].reshape(KL, P, 2 * QKH).transpose(1, 0, 2).reshape(P, -1)
        units.append(np.concatenate([u, np.zeros((P, UNIT - u.shape[1]), u.dtype)], 1))
        add(f("mla_w_ukv")[0][:, g * 2 * (NOPE + VH):(g + 1) * 2 * (NOPE + VH)], KL, 2 * (NOPE + VH))
    blocks(f("mla_w_o")[0])
    gate(0)
    w = f("ssd_w_in")[0]
    z0, x0, b0, c0, d0 = 0, DI, 2 * DI, 2 * DI + NG * NS, 2 * DI + 2 * NG * NS
    add(w[:, d0:], KD, 2 * NH)
    for g in range(NG):
        blocks(w[:, x0 + g * BLK:x0 + (g + 1) * BLK])
        add(np.concatenate([w[:, b0 + g * NS:b0 + (g + 1) * NS], w[:, c0 + g * NS:c0 + (g + 1) * NS]], 1), KD, 2 * NS)
        blocks(w[:, z0 + g * BLK:z0 + (g + 1) * BLK])
    w = f("ssd_w_out")[0]
    for c in range(NB):
        order = Y_ORDER if c else Y_FIRST
        blocks(w[np.concatenate([np.arange(k * P, (k + KU) * P) for k in order]), c * BLK:(c + 1) * BLK])
    gate(1)
    units += [np.zeros((P, UNIT), np.float32)] * 2
    return np.stack(units)


def kernel(**inputs):
    import concourse.bacc as bacc
    from concourse.bass_utils import run_bass_kernel_spmd

    arrays = layout_all(inputs)
    nc = bacc.Bacc("TRN2", target_bir_lowering=False, num_devices=1)
    args = [nc.dram_tensor(n, a.shape, mybir.dt.from_np(a.dtype), kind="ExternalInput").ap() for n, a in arrays.items()]
    out = nc.dram_tensor("out_dram", (SEQ, D), F32, kind="ExternalOutput").ap()
    trunk(nc, *args, out)
    r = run_bass_kernel_spmd(nc, [arrays], core_ids=[0])
    return r.results[0]["out_dram"].reshape(1, SEQ, D)


def layout_all(inputs):
    f = lambda n: np.asarray(inputs[n])
    a = np.arange(P)
    consts = np.stack([np.eye(P), a[:, None] <= a[None, :], a[:, None] >= a[None, :], np.ones((P, P))]).astype(np.float32)
    invf = 1.0 / (np.float32(10000.0) ** (np.arange(0, ROPE, 2, dtype=np.float32) / np.float32(ROPE)))
    chunks = lambda v: v.reshape(-1, P).T
    small = np.concatenate([chunks(f("mla_q_norm")[0]), chunks(f("mla_kv_norm")[0]), chunks(f("ssd_norm")[0])], 1)
    lnw = np.stack([f("ln_g")[0], f("ln_b")[0], f("ln_g")[1], f("ln_b")[1]])
    convw = np.concatenate([f("ssd_conv_w")[0], f("ssd_conv_b")[0][None]], 0)
    convw = convw.reshape(TAPS + 1, -1, P).transpose(2, 1, 0)
    rows = np.concatenate([invf, f("ssd_dt_bias")[0].ravel(), f("ssd_a_log")[0].ravel(), f("ssd_d")[0]])[None]
    return {
        "x_dram": f("x")[0], "p_dram": f("p")[:, 0], "pos_dram": np.ascontiguousarray(f("positions").reshape(TT, P).T),
        "consts_dram": consts, "ln_dram": lnw, "weights_dram": layout(inputs), "small_dram": np.ascontiguousarray(small),
        "conv_dram": np.ascontiguousarray(convw), "rows_dram": rows,
    }
```
